# Optimizing a Trainium2 kernel written in Bass

```python
import jax, jax.numpy as jnp
from jax import lax
import numpy as np

D_MODEL = 1024
BATCH = 1
SEQ = 256
DEPTH = 2

N_MEM = 256
EPS = 1e-6
ROPE_THETA = 10000.0
ATT_HEADS = 8
ATT_KV_HEADS = 2
ATT_HEAD_DIM = D_MODEL // ATT_HEADS
IDX_HEADS = 4
IDX_DIM = 64
TOPK_MAX = 256
Q_BLOCK = 128
GDN_HEADS = 8
GDN_DK = 128
GDN_DV = 128
CONV_K = 4
CHUNK = 64
XATT_HEADS = 4
XATT_HEAD_DIM = D_MODEL // XATT_HEADS
FF_DIM = -(-8 * D_MODEL // (3 * 256)) * 256

A_Q = ATT_HEADS * ATT_HEAD_DIM
A_KV = ATT_KV_HEADS * ATT_HEAD_DIM
I_Q = IDX_HEADS * IDX_DIM
I_K = IDX_DIM
I_W = IDX_HEADS
B_QK = GDN_HEADS * GDN_DK
B_V = GDN_HEADS * GDN_DV
B_QKV = 2 * B_QK + B_V
B_A = GDN_HEADS
B_B = GDN_HEADS
G_A = A_Q
G_B = B_V
IN_SPLITS = (A_Q, A_KV, A_KV, I_Q, I_K, I_W, B_QKV, B_A, B_B, G_A, G_B)
IN_COLS = A_Q + 2 * A_KV + I_Q + I_K + I_W + B_QKV + B_A + B_B + G_A + G_B

kernel_name = "hybrid_dsa_gdn_parallel_block"

def _split_points(sizes):
    return [int(v) for v in np.cumsum(sizes)[:-1]]

def _rms_norm(x, g):
    xf = x.astype(jnp.float32)
    y = xf * lax.rsqrt(jnp.mean(xf * xf, axis=-1, keepdims=True) + EPS)
    return (y * g.astype(jnp.float32)).astype(x.dtype)

def _l2norm(x):
    return x * lax.rsqrt(jnp.sum(x * x, axis=-1, keepdims=True) + EPS)

def _rope(x, positions):
    d = x.shape[-1]
    half = d // 2
    inv_freq = ROPE_THETA ** (-jnp.arange(half, dtype=jnp.float32) * 2.0 / d)
    ang = positions.astype(jnp.float32)[:, :, None] * inv_freq
    cos = jnp.cos(ang)[:, :, None, :]
    sin = jnp.sin(ang)[:, :, None, :]
    xf = x.astype(jnp.float32)
    x1, x2 = xf[..., :half], xf[..., half:]
    return jnp.concatenate([x1 * cos - x2 * sin, x2 * cos + x1 * sin], axis=-1).astype(x.dtype)

def _dsa_attention(q, k, v, q_idx, k_idx, w_idx, topk):
    B, S, H, Dh = q.shape
    G = ATT_KV_HEADS
    R = H // G
    n_blk = S // Q_BLOCK

    def to_blocks(a):
        return jnp.swapaxes(a.reshape((B, n_blk, Q_BLOCK) + a.shape[2:]), 0, 1)

    starts = jnp.arange(n_blk, dtype=jnp.int32) * Q_BLOCK
    key_pos = jnp.arange(S, dtype=jnp.int32)
    k_idx_f = k_idx.astype(jnp.float32)
    scale = Dh ** -0.5
    idx_scale = IDX_DIM ** -0.5

    def one_block(args):
        qb, qib, wb, t0 = args
        t_pos = t0 + jnp.arange(Q_BLOCK, dtype=jnp.int32)
        logits = jnp.einsum('bthd,bsd->bths', qib.astype(jnp.float32), k_idx_f) * idx_scale
        score = jnp.einsum('bth,bths->bts', wb.astype(jnp.float32), jax.nn.relu(logits))
        causal = key_pos[None, :] <= t_pos[:, None]
        score = jnp.where(causal[None], score, -jnp.inf)
        _, sel = lax.top_k(score, topk)
        valid = sel <= t_pos[None, :, None]
        kg = jax.vmap(lambda a, i: a[i])(k, sel)
        vg = jax.vmap(lambda a, i: a[i])(v, sel)
        qg = qb.reshape(B, Q_BLOCK, G, R, Dh).astype(jnp.float32)
        s = jnp.einsum('btgrd,btngd->btgrn', qg, kg.astype(jnp.float32)) * scale
        s = jnp.where(valid[:, :, None, None, :], s, -jnp.inf)
        p = jax.nn.softmax(s, axis=-1)
        o = jnp.einsum('btgrn,btngd->btgrd', p, vg.astype(jnp.float32))
        return o.reshape(B, Q_BLOCK, H * Dh).astype(q.dtype)

    out = lax.map(one_block, (to_blocks(q), to_blocks(q_idx), to_blocks(w_idx), starts))
    return jnp.swapaxes(out, 0, 1).reshape(B, S, H * Dh)

def _causal_conv_silu(x, w):
    K = w.shape[0]
    S = x.shape[1]
    xp = jnp.pad(x, ((0, 0), (K - 1, 0), (0, 0)))
    y = xp[:, 0:S] * w[0]
    for j in range(1, K):
        y = y + xp[:, j:j + S] * w[j]
    return jax.nn.silu(y)

def _gated_delta_rule(q, k, v, g, beta):
    B, S, H, Dk = q.shape
    Dv = v.shape[-1]
    C = CHUNK
    N = S // C

    def chunks(a):
        a = a.reshape((B, N, C, H) + a.shape[3:])
        return jnp.moveaxis(a, 3, 1)

    q = chunks(q) * (Dk ** -0.5)
    k = chunks(k)
    v = chunks(v)
    g = chunks(g)
    beta = chunks(beta)
    g_cum = jnp.cumsum(g, axis=-1)
    tril = jnp.tril(jnp.ones((C, C), dtype=bool))
    strict = jnp.tril(jnp.ones((C, C), dtype=bool), -1)
    diff = g_cum[..., :, None] - g_cum[..., None, :]
    decay = jnp.where(tril, jnp.exp(jnp.where(tril, diff, 0.0)), 0.0)
    k_beta = k * beta[..., None]
    v_beta = v * beta[..., None]
    m = jnp.where(strict, jnp.einsum('bhnid,bhnjd->bhnij', k_beta, k) * decay, 0.0)
    a_mat = m + jnp.eye(C, dtype=jnp.float32)
    rhs = jnp.concatenate([v_beta, k_beta * jnp.exp(g_cum)[..., None]], axis=-1)
    sol = lax.linalg.triangular_solve(a_mat, rhs, left_side=True, lower=True, unit_diagonal=True)
    u = sol[..., :Dv]
    w = sol[..., Dv:]
    attn = jnp.einsum('bhnid,bhnjd->bhnij', q, k) * decay
    q_dec = q * jnp.exp(g_cum)[..., None]
    k_dec = k * jnp.exp(g_cum[..., -1:] - g_cum)[..., None]
    g_last = jnp.exp(g_cum[..., -1])

    def step(state, xs):
        u_c, w_c, attn_c, qd_c, kd_c, gl_c = xs
        v_new = u_c - jnp.einsum('bhcd,bhde->bhce', w_c, state)
        o = jnp.einsum('bhcd,bhde->bhce', qd_c, state) + jnp.einsum('bhij,bhje->bhie', attn_c, v_new)
        state = state * gl_c[..., None, None] + jnp.einsum('bhcd,bhce->bhde', kd_c, v_new)
        return state, o

    xs = (jnp.moveaxis(u, 2, 0), jnp.moveaxis(w, 2, 0), jnp.moveaxis(attn, 2, 0),
          jnp.moveaxis(q_dec, 2, 0), jnp.moveaxis(k_dec, 2, 0), jnp.moveaxis(g_last, 2, 0))
    state0 = jnp.zeros((B, H, Dk, Dv), dtype=jnp.float32)
    _, o = lax.scan(step, state0, xs)
    return jnp.transpose(o, (1, 0, 3, 2, 4)).reshape(B, S, H, Dv)

def _hybrid_mixer(h, positions, w_in, conv_w, a_log, dt_bias, gdn_norm, w_out, topk):
    B, S, _ = h.shape
    proj = h @ w_in
    (a_q, a_k, a_v, i_q, i_k, i_w, b_qkv, b_a, b_b, g_a, g_b) = jnp.split(
        proj, _split_points(IN_SPLITS), axis=-1)

    q = _rope(a_q.reshape(B, S, ATT_HEADS, ATT_HEAD_DIM), positions)
    k = _rope(a_k.reshape(B, S, ATT_KV_HEADS, ATT_HEAD_DIM), positions)
    v = a_v.reshape(B, S, ATT_KV_HEADS, ATT_HEAD_DIM)
    qi = _rope(i_q.reshape(B, S, IDX_HEADS, IDX_DIM), positions)
    ki = _rope(i_k.reshape(B, S, 1, IDX_DIM), positions)[:, :, 0]
    wi = i_w * (IDX_HEADS ** -0.5)
    y_a = _dsa_attention(q, k, v, qi, ki, wi, topk)

    qkv = _causal_conv_silu(b_qkv, conv_w)
    bq, bk, bv = jnp.split(qkv, [B_QK, 2 * B_QK], axis=-1)
    bq = _l2norm(bq.astype(jnp.float32).reshape(B, S, GDN_HEADS, GDN_DK))
    bk = _l2norm(bk.astype(jnp.float32).reshape(B, S, GDN_HEADS, GDN_DK))
    bv = bv.astype(jnp.float32).reshape(B, S, GDN_HEADS, GDN_DV)
    g = -jnp.exp(a_log.astype(jnp.float32)) * jax.nn.softplus(
        b_a.astype(jnp.float32) + dt_bias.astype(jnp.float32))
    beta = jax.nn.sigmoid(b_b.astype(jnp.float32))
    o_b = _gated_delta_rule(bq, bk, bv, g, beta)
    y_b = _rms_norm(o_b, gdn_norm).reshape(B, S, B_V).astype(h.dtype)

    y = jax.nn.sigmoid(g_a) * y_a + jax.nn.sigmoid(g_b) * y_b
    return y @ w_out

def _memory_cross_attention(h, mem_n, w_xq, w_xkv, w_xo):
    B, S, _ = h.shape
    M = mem_n.shape[1]
    q = (h @ w_xq).reshape(B, S, XATT_HEADS, XATT_HEAD_DIM)
    kv = mem_n @ w_xkv
    k, v = jnp.split(kv, 2, axis=-1)
    k = k.reshape(B, M, XATT_HEADS, XATT_HEAD_DIM)
    v = v.reshape(B, M, XATT_HEADS, XATT_HEAD_DIM)
    s = jnp.einsum('bshd,bmhd->bhsm', q.astype(jnp.float32), k.astype(jnp.float32)) * (XATT_HEAD_DIM ** -0.5)
    p = jax.nn.softmax(s, axis=-1)
    o = jnp.einsum('bhsm,bmhd->bshd', p, v.astype(jnp.float32)).astype(h.dtype)
    return o.reshape(B, S, D_MODEL) @ w_xo

def _swiglu(h, w_gu, w_down):
    gate, up = jnp.split(h @ w_gu, 2, axis=-1)
    return (jax.nn.silu(gate) * up) @ w_down

def setup_inputs(seed: int = 0) -> dict:
    key = jax.random.key(seed)
    ks = jax.random.split(key, 24)
    f32 = jnp.float32

    def dense(k, shape, fan_in):
        return jax.random.normal(k, shape, f32) * (fan_in ** -0.5)

    def gain(k):
        return 1.0 + 0.02 * jax.random.normal(k, (DEPTH, D_MODEL), f32)

    x = jax.random.normal(ks[0], (BATCH, SEQ, D_MODEL), f32)
    mem = jax.random.normal(ks[1], (BATCH, N_MEM, D_MODEL), f32)
    offsets = jax.random.randint(ks[2], (BATCH, 1), 0, 1024, dtype=jnp.int32)
    positions = offsets + jnp.arange(SEQ, dtype=jnp.int32)[None, :]
    dt = jnp.exp(jax.random.uniform(ks[6], (DEPTH, GDN_HEADS), f32,
                                    jnp.log(0.001), jnp.log(0.1)))
    return {
        "x": x,
        "mem": mem,
        "positions": positions,
        "norm_mix_pre": gain(ks[3]),
        "w_in": dense(ks[4], (DEPTH, D_MODEL, IN_COLS), D_MODEL),
        "conv_w": 0.5 * jax.random.normal(ks[5], (DEPTH, CONV_K, B_QKV), f32),
        "a_log": jnp.log(jax.random.uniform(ks[7], (DEPTH, GDN_HEADS), f32, 1.0, 16.0)),
        "dt_bias": dt + jnp.log(-jnp.expm1(-dt)),
        "gdn_norm": 1.0 + 0.02 * jax.random.normal(ks[8], (DEPTH, GDN_DV), f32),
        "w_out": dense(ks[9], (DEPTH, A_Q, D_MODEL), A_Q),
        "norm_mix_post": gain(ks[10]),
        "norm_x_pre": gain(ks[11]),
        "norm_mem": gain(ks[12]),
        "w_xq": dense(ks[13], (DEPTH, D_MODEL, D_MODEL), D_MODEL),
        "w_xkv": dense(ks[14], (DEPTH, D_MODEL, 2 * D_MODEL), D_MODEL),
        "w_xo": dense(ks[15], (DEPTH, D_MODEL, D_MODEL), D_MODEL),
        "norm_x_post": gain(ks[16]),
        "norm_ffn_pre": gain(ks[17]),
        "w_gu": dense(ks[18], (DEPTH, D_MODEL, 2 * FF_DIM), D_MODEL),
        "w_down": dense(ks[19], (DEPTH, FF_DIM, D_MODEL), FF_DIM),
        "norm_ffn_post": gain(ks[20]),
    }

def reference(x, mem, positions, norm_mix_pre, w_in, conv_w, a_log, dt_bias, gdn_norm, w_out,
              norm_mix_post, norm_x_pre, norm_mem, w_xq, w_xkv, w_xo, norm_x_post,
              norm_ffn_pre, w_gu, w_down, norm_ffn_post):
    S = x.shape[1]
    topk = min(TOPK_MAX, S // 4)
    for l in range(DEPTH):
        h = _rms_norm(x, norm_mix_pre[l])
        y = _hybrid_mixer(h, positions, w_in[l], conv_w[l], a_log[l], dt_bias[l], gdn_norm[l],
                          w_out[l], topk)
        x = x + _rms_norm(y, norm_mix_post[l])
        h = _rms_norm(x, norm_x_pre[l])
        mem_n = _rms_norm(mem, norm_mem[l])
        y = _memory_cross_attention(h, mem_n, w_xq[l], w_xkv[l], w_xo[l])
        x = x + _rms_norm(y, norm_x_post[l])
        h = _rms_norm(x, norm_ffn_pre[l])
        y = _swiglu(h, w_gu[l], w_down[l])
        x = x + _rms_norm(y, norm_ffn_post[l])
    return x


_drawn_inputs = setup_inputs


def setup_inputs(seed=0):
    import zlib

    import numpy as np

    out = dict(_drawn_inputs(seed))
    spreads = {}
    factors = {'norm_x_pre': 3.009, 'norm_x_post': 2.948, 'norm_ffn_post': 3.622}
    for name, (base, spread) in spreads.items():
        noise = np.random.default_rng([zlib.crc32(name.encode()), seed]).standard_normal(out[name].shape)
        drawn = base * np.exp(spread * noise) if base else spread * noise
        out[name] = __import__('jax').numpy.asarray(drawn.astype(out[name].dtype))
    for name, factor in factors.items():
        out[name] = (out[name] * factor).astype(out[name].dtype)
    return out
```

```python
from contextlib import ExitStack

import numpy as np

import concourse.bass as bass
from concourse import mybir

ALU = mybir.AluOpType
ACT = mybir.ActivationFunctionType
AX_X = mybir.AxisListType.X
F32 = mybir.dt.float32
BF16 = mybir.dt.bfloat16
I32 = mybir.dt.int32

P = 128
D = 1024
KT = D // P
S = 256
TILES = S // P
DEPTH = 2
EPS = 1e-6
THETA = 10000.0
HEADS, KV_HEADS, DH = 8, 2, 128
IDX_HEADS, IDX_DIM = 4, 64
TOPK = min(256, S // 4)
CONV_K = 4
G_HEADS = 8
X_HEADS = 4
X_DH = D // X_HEADS
FF = -(-8 * D // (3 * 256)) * 256
FF_BLOCKS = FF // P
NEG = -1.0e30
TAKEN = -3.0e38

SIZES = dict(q=HEADS * DH, k=KV_HEADS * DH, v=KV_HEADS * DH, iq=IDX_HEADS * IDX_DIM, ik=IDX_DIM, iw=IDX_HEADS,
             bq=D, bk=D, bv=D, ba=G_HEADS, bb=G_HEADS, ga=D, gb=D)
COL = dict(zip(SIZES, np.cumsum([0] + list(SIZES.values())[:-1]).tolist()))

SLOT = KT * 256
STREAM = (
    [("xk", i) for i in range(4)] + [("iq", 0), ("small", 0), ("k", 0), ("v", 0)]
    + [("q", i) for i in range(4)]
    + [("bk", i) for i in range(4)] + [("bq", i) for i in range(4)] + [("bv", i) for i in range(4)]
    + [("ga", i) for i in range(4)] + [("gb", i) for i in range(4)]
    + [("out", i) for i in range(4)] + [("xv", i) for i in range(4)]
    + [("xq", i) for i in range(4)] + [("xo", i) for i in range(4)]
    + [(part, i) for i in range(FF // 256) for part in ("gate", "up")]
    + [("down", i) for i in range(FF_BLOCKS // 2)]
)
SLOTS = len(STREAM)
RING = 3
assert SLOTS % RING == 0
SLOT_AT = {key: n for n, key in enumerate(STREAM)}

C_IDENT, C_AFTER, C_UPTO, C_MASK1, C_IDXBIAS = 0, 128, 256, 384, 512
C_LEVEL = 640
LEVELS = (2, 4, 8, 16, 32, 64)
C_INV_A = C_LEVEL + 64 * len(LEVELS)
C_INV_I, C_SGN_A, C_SGN_I, C_ONE = C_INV_A + 1, C_INV_A + 2, C_INV_A + 3, C_INV_A + 4
C_EPS = C_ONE + 1
C_NEGHALF = C_EPS + 1
N_CONST = C_NEGHALF + 16
R_CONV, R_MIX, R_X, R_MEM, R_FFN, R_GDN, R_DT, R_ALOG = 0, 96, 104, 112, 120, 128, 129, 137
N_PARAM = 145

PI = 3.141592653589793
TWO_PI_1 = 6.28125
TWO_PI_2 = 2029.0 / 2 ** 20
TWO_PI_3 = 2 * PI - TWO_PI_1 - TWO_PI_2
PI_BELOW = 3.1415925
ROUND = 12582912.0


class Plan:

    def __init__(self):
        self.marks, self.totals, self.banks = {}, {}, {}


class Steps:

    def __init__(self, plan, sem, name):
        self.plan, self.sem, self.name, self.count = plan, sem, name, 0

    def mark(self, what):
        self.count += 1
        self.plan.marks[self.name, what] = self.count
        self.plan.totals[self.name] = max(self.count, self.plan.totals.get(self.name, 0))
        return 1

    def at(self, layer, what):
        return self.sem, layer * self.plan.totals.get(self.name, 1) + self.plan.marks.get((self.name, what), 1)


def program(nc, plan, x_in, mem_in, pos_in, weights, params, post_gains, consts, consts_b, out):
    with ExitStack() as ctx:
        def sb(name, cols, dt=F32):
            return ctx.enter_context(nc.sbuf_tensor(f"sb_{name}", [P, cols], dt))

        def steps(name):
            return Steps(plan, ctx.enter_context(nc.semaphore(name)), name)

        def sem(name):
            return ctx.enter_context(nc.semaphore(name))

        ring_t = sb("ring", RING * SLOT)
        x_t = sb("x", TILES * D)
        mem_feat_t = sb("mem_feat", D * TILES)
        mem_gain_t = sb("mem_gain", D * TILES)
        kx_t = sb("kx", D * TILES)
        vx_t = sb("vx", D * TILES)
        rope_t = sb("rope_tables", 4 * S)
        const_t = sb("const", N_CONST)
        constb_t = sb("const_b", 5 * P, BF16)
        param_t = sb("param", N_PARAM)
        gain_t = sb("post_gain", D)
        h_t = sb("h", D * TILES)
        y_t = sb("y", D * TILES)
        gates_t = sb("gates", 2 * D * TILES)
        conv_t = sb("conv", 3 * D * TILES)
        th_t = sb("th", 1024)
        sq_t = sb("sq", 1024)
        decay_t = sb("decay", 2048)
        attn_t = sb("attn", 2048)
        m_t = sb("m", 2048)
        ra_t = sb("region_a", 2048)
        rb_t = sb("region_b", 2048)
        rc_t = sb("region_c", 1024)
        kd_t = sb("k_rope", KV_HEADS * S)
        v_t = sb("v", KV_HEADS * S)
        selb_t = sb("sel_bias", TILES * S, BF16)
        tiny_t = sb("tiny", 512)
        psum = ctx.enter_context(nc.psum_tensor("psum", [P, 8, 512], F32))

        ring = ring_t[:, :].rearrange("p (r n) -> p r n", r=RING)
        x = x_t[:, :].rearrange("p (c d) -> p c d", c=TILES)
        feat = lambda t: t[:, 0:D * TILES].rearrange("p (k t) -> p k t", t=S)
        mem_feat, mem_gain, kx, h, y = feat(mem_feat_t), feat(mem_gain_t), feat(kx_t), feat(h_t), feat(y_t)
        vx = vx_t[:, :].rearrange("p (c d) -> p c d", c=TILES)
        rope = rope_t[:, :].rearrange("p (w t) -> p w t", w=4)
        ident = const_t[:, C_IDENT:C_IDENT + P]
        after = const_t[:, C_AFTER:C_AFTER + P]
        upto = const_t[:, C_UPTO:C_UPTO + P]
        mask1 = const_t[:, C_MASK1:C_MASK1 + P]
        idx_bias = const_t[:, C_IDXBIAS:C_IDXBIAS + P]
        one = const_t[:, C_ONE:C_ONE + 1]
        eps_col = const_t[:, C_EPS:C_EPS + 1]
        neghalf = const_t[:, C_NEGHALF:C_NEGHALF + 16]
        ident_b = constb_t[:, 0:P]
        decay_bias = constb_t[:, P:5 * P]
        gates = gates_t[:, :].rearrange("p (k t) -> p k t", t=S)
        conv = conv_t[:, :].rearrange("p (k t) -> p k t", t=S)
        th = th_t[:, :].rearrange("p (b n) -> p b n", b=2)
        sq = sq_t[:, :].rearrange("p (b n) -> p b n", b=2)
        grp = lambda t: t[:, 0:2048].rearrange("p (g h n) -> p g h n", g=4, h=4)
        decay, attn, m_up = grp(decay_t), grp(attn_t), grp(m_t)
        xn = ra_t[:, :].rearrange("p (c d) -> p c d", c=TILES)
        idx_relu = ra_t[:, 0:1024].rearrange("p (h s) -> p h s", h=IDX_HEADS)
        idx_val = ra_t[:, 1024:1536].rearrange("p (c s) -> p c s", c=TILES)
        iq = rb_t[:, 0:512].rearrange("p (b t) -> p b t", b=2)
        ik = rb_t[:, 512:768]
        rope_tmp = rc_t[:, 0:1024].rearrange("p (b n) -> p b n", b=2)
        p1 = ra_t[:, :].rearrange("p (h s) -> p h s", h=HEADS)
        t_up = grp(ra_t)
        q = gates_t[:, 0:2048].rearrange("p (h t) -> p h t", h=HEADS)
        pt0 = rb_t[:, :].rearrange("p (h t) -> p h t", h=HEADS)
        t_low = grp(rb_t)
        p0 = y_t[:, 0:1024].rearrange("p (h s) -> p h s", h=HEADS)
        pt1 = rc_t[:, :].rearrange("p (h t) -> p h t", h=HEADS)
        prod = rc_t[:, :].rearrange("p (g h n) -> p g h n", g=4, h=4)
        g_after = vx_t[:, :].rearrange("p (c h n) -> p c h n", c=TILES, h=G_HEADS)
        rhs = grp(vx_t)
        v_new = grp(decay_t)
        k_dec = h_t[:, 0:1024].rearrange("p (h n) -> p h n", h=G_HEADS)
        state = h_t[:, 1024:2048].rearrange("p (h n) -> p h n", h=G_HEADS)
        o_tok = grp(m_t)
        kT = kd_t[:, :].rearrange("p (g t) -> p g t", g=KV_HEADS)
        v_tok = v_t[:, :].rearrange("p (c d) -> p c d", c=TILES)
        sel_bias = selb_t[:, :].rearrange("p (c s) -> p c s", c=TILES)
        qx = gates_t[:, 0:2048].rearrange("p (k t) -> p k t", t=S)
        px = gates_t[:, 2048:4096].rearrange("p (c h s) -> p c h s", c=TILES, h=X_HEADS)
        pxt = decay_t[:, :].rearrange("p (b h t) -> p b h t", b=TILES, h=X_HEADS)
        ox = feat(attn_t)
        ff = conv_t[:, 0:FF_BLOCKS * S].rearrange("p (k t) -> p k t", t=S)

        tiny_at = [0]

        def tiny(n):
            tiny_at[0] += n
            assert tiny_at[0] <= 512
            return tiny_t[:, tiny_at[0] - n:tiny_at[0]]

        ss, rs = tiny(2), tiny(2)
        ss2, rs2 = tiny(2), tiny(2)
        small = tiny(2 * 20).rearrange("p (c n) -> p c n", c=TILES)
        two = lambda: tiny(16).rearrange("p (c h) -> p c h", c=TILES)
        ga_x, ga_abs, ga_e, ga_w, ga_ln, ga_t, ga_r, g_tok, beta = (two() for _ in range(9))
        a_exp = tiny(8)
        top8 = tiny(8)
        e_last, e_cum = tiny(8), tiny(8)
        ss_kq = tiny(32).rearrange("p (c b) -> p c b", c=TILES)
        rk, v_scale, d_k, m_scale, o_eps, k_scale0 = two(), two(), two(), two(), two(), tiny(8)
        half_gdn = tiny(1)
        mx, nmx, psumr, pinv = (tiny(16).rearrange("p (c h) -> p c h", c=TILES) for _ in range(4))
        oss, oscale = two(), two()

        ring_loaded = [sem(f"ring_loaded_{k}") for k in range(RING)]
        consts_loaded, x_loaded, mem_loaded, pos_loaded = (sem(f"{n}_loaded") for n in ("consts", "x", "mem", "pos"))
        tables_act = sem("tables_act")
        mem_act, mem_pool, mem_dve, mem_pe = (sem(f"mem_{n}") for n in ("act", "pool", "dve", "pe"))
        out_stored = sem("out_stored")
        param_loaded = sem("param_loaded")
        gain_loaded = sem("gain_loaded")
        slots = steps("slots")
        pe_t = steps("pe_transposed")
        pe_idx = steps("pe_idx")
        pe_att = steps("pe_att")
        pe_gdn = steps("pe_gdn")
        pe_x = steps("pe_xattn")
        pe_out = steps("pe_out_tile0")
        act_norm = steps("act_norm")
        act_copy = steps("act_copy")
        act_gate = steps("act_gate")
        act_conv = steps("act_conv")
        act_att = steps("act_att")
        act_gdn = steps("act_gdn")
        act_ff = steps("act_ff")
        dve_norm = steps("dve_norm")
        dve_rope = steps("dve_rope")
        dve_gate = steps("dve_gate")
        dve_idx = steps("dve_idx")
        dve_conv = steps("dve_conv")
        dve_att = steps("dve_att")
        dve_gdn = steps("dve_gdn")
        dve_ff = steps("dve_ff")
        pool_norm = steps("pool_norm")
        mem_gain_ready = sem("mem_gain_ready")
        x_ready = sem("x_ready")
        table = steps("table")
        pool_gdn = steps("pool_gdn")

        def bank(what):
            return psum[:, plan.banks.get(what, 0), :]

        def angle(w):
            return y_t[:, (2 + w) * S:(3 + w) * S]

        def tap(k, block):
            col = R_CONV + 24 * k + block
            return param_t[:, col:col + 1]

        def y_tile(c):
            return psum[:, 4 + 2 * c:6 + 2 * c, :].rearrange("p b n -> p (b n)")

        def cols(ap, n):
            m = ap.shape[-1]
            return ap.unsqueeze(2).broadcast_to([P, m, n])

        def heads(ap, m):
            return ap.unsqueeze(1).broadcast_to([P, m, ap.shape[-1]])

        def even(t, s):
            return t.rearrange("p h (b w c) -> p (h b) w c", w=2, c=s)[:, :, 0, :]

        block = ctx.enter_context(nc.Block())

        @block.sync
        def _(sp):
            sp.dma_start(mem_block(kx_t), mem_in.rearrange("(c p) d -> p c d", p=P)).then_inc(mem_loaded, 16)
            sp.dma_start(const_t[:, :], consts).then_inc(consts_loaded, 16)
            sp.dma_start(constb_t[:, :], consts_b).then_inc(consts_loaded, 16)
            sp.dma_start(x, x_in.rearrange("(c p) d -> p c d", p=P)).then_inc(x_loaded, 16)
            sp.dma_start(y_t[:, 0:S].bitcast(I32), pos_in.broadcast_to([P, S])).then_inc(pos_loaded, 16)
            for k in range(RING):
                sp.dma_start(ring[:, k, :], weights[k]).then_inc(ring_loaded[k], 16)
            with sp.Fori(1, DEPTH * SLOTS // RING) as r:
                for k in range(RING):
                    sp.wait_ge(slots.sem, (r - 1) * RING + k + 1)
                    sp.dma_start(ring[:, k, :], weights[bass.ds(r * RING + k, 1), :, :].rearrange("a p n -> p (a n)"))\
                        .then_inc(ring_loaded[k], 16)
            sp.wait_ge(x_ready, TILES * (DEPTH + 1))
            sp.dma_start(out.rearrange("(c p) d -> p c d", p=P), x).then_inc(out_stored, 16)
            sp.wait_ge(out_stored, 16)

        @block.tensor
        def _(pe):
            pe.wait_ge(consts_loaded, 32)
            for j in range(4):
                c, half = j // 2, j % 2
                pe.wait_ge(mem_dve, c + 1)
                for k in range(4):
                    tr = pe.transpose(psum[:, j, k * P:(k + 1) * P], mem_block(kx_t)[:, c, (4 * half + k) * P:(4 * half + k + 1) * P], ident)
                tr.then_inc(mem_pe, 1)

            with pe.Fori(0, DEPTH) as layer:
                last = {}
                turn = [0]

                def claim(what, reader, banks=range(7)):
                    b = min(banks, key=lambda b: ((b - turn[0]) % 8))
                    turn[0] = (b + 1) % 8
                    if b in last:
                        pe.wait_ge(*last[b][0].at(layer, last[b][1]))
                    last[b] = reader
                    plan.banks[what] = b
                    return psum[:, b, :]

                def weights_here(n):
                    pe.wait_ge(ring_loaded[n % RING], 16 * (layer * (SLOTS // RING) + n // RING + 1))
                    return ring[:, n % RING, :]

                def wide(key, act, reader, banks=range(7)):
                    n = SLOT_AT[key]
                    o = claim(key, reader, banks)
                    w = weights_here(n).rearrange("p (k n) -> p k n", k=KT)
                    for b in range(2):
                        for k in range(KT):
                            mm = pe.matmul(o[:, b * S:(b + 1) * S], w[:, k, b * P:(b + 1) * P], act[:, k, :],
                                           start=(k == 0), stop=(k == KT - 1))
                    mm.then_inc(slots.sem, slots.mark(key))

                def halves(part, act, outs):
                    for i in range(4):
                        half, khalf = i // 2, i % 2
                        w = weights_here(SLOT_AT[part, i]).rearrange("p (k n) -> p k n", k=4)
                        for c in range(TILES):
                            for k in range(4):
                                mm = pe.matmul(outs[c][half], act[:, 4 * khalf + k, c * P:(c + 1) * P], w[:, k, :],
                                               start=(khalf == 0 and k == 0), stop=(khalf == 1 and k == 3))
                            if c == 0 and i == 3:
                                mm.then_inc(pe_out.sem, pe_out.mark(part))
                        mm.then_inc(slots.sem, slots.mark((part, i)))

                def norm_transposes(which):
                    for c in range(TILES):
                        pe.wait_ge(*dve_norm.at(layer, ("xn", which, c)))
                        for half in range(2):
                            what = ("h", which, c, half)
                            o = claim(what, (dve_norm, what), range(4))
                            for k in range(4):
                                b = 4 * half + k
                                tr = pe.transpose(o[:, k * P:(k + 1) * P], xn[:, c, b * P:(b + 1) * P], ident)
                            tr.then_inc(pe_t.sem, pe_t.mark(what))

                pe.wait_ge(mem_gain_ready, layer + 1)
                for i in range(4):
                    wide(("xk", i), mem_gain, (act_copy, ("xk", i)), range(4))
                norm_transposes("mix")
                pe.wait_ge(*dve_norm.at(layer, ("h", "mix", 1, 1)))
                wide(("iq", 0), h, (dve_rope, "iq"))
                n = SLOT_AT["small", 0]
                o = claim(("small", 0), (act_copy, "small"))
                w = weights_here(n).rearrange("p (k n) -> p k n", k=KT)
                for k in range(KT):
                    pe.matmul(o[:, 0:S], w[:, k, 0:P], h[:, k, :], start=(k == 0), stop=(k == KT - 1))
                for c in range(TILES):
                    for k in range(KT):
                        mm = pe.matmul(o[:, S + 20 * c:S + 20 * c + 20], h[:, k, c * P:(c + 1) * P], w[:, k, P:P + 20],
                                       start=(k == 0), stop=(k == KT - 1))
                mm.then_inc(slots.sem, slots.mark(("small", 0)))
                wide(("k", 0), h, (dve_rope, "k"))
                n = SLOT_AT["v", 0]
                o = claim(("v", 0), (act_copy, "v"))
                w = weights_here(n).rearrange("p (k n) -> p k n", k=KT)
                for c in range(TILES):
                    for k in range(KT):
                        mm = pe.matmul(o[:, c * 256:(c + 1) * 256], h[:, k, c * P:(c + 1) * P], w[:, k, :],
                                       start=(k == 0), stop=(k == KT - 1))
                mm.then_inc(slots.sem, slots.mark(("v", 0)))
                wide(("q", 0), h, (dve_rope, ("q", 0)))
                pe.wait_ge(*dve_rope.at(layer, "iq"))
                pe.wait_ge(*dve_rope.at(layer, "ik"))
                for c in range(TILES):
                    keys = (c + 1) * P
                    for odd in range(2):
                        what = ("logits", c, odd)
                        o = claim(what, (act_att, what))
                        lo = 64 * odd
                        for b in range(2):
                            mm = pe.matmul(o[:, b * keys:(b + 1) * keys], iq[lo:lo + 64, b, c * P:(c + 1) * P],
                                           ik[lo:lo + 64, 0:keys], start=True, stop=True)
                        mm.then_inc(pe_idx.sem, pe_idx.mark(what))
                for i in range(1, 4):
                    wide(("q", i), h, (dve_rope, ("q", i)))
                misc = psum[:, 7, :]
                last[7] = (dve_gdn, "ss")
                for c in range(TILES):
                    pe.wait_ge(*dve_gate.at(layer, ("g_after", c)))
                    for hh in range(2):
                        what = ("decay", c, hh)
                        o = claim(what, (act_gdn, what))
                        pe.matmul(o, ident_b, decay_bias, start=True, stop=False, skip_group_check=True)
                        for hd in range(4):
                            mm = pe.matmul(o[:, hd * P:(hd + 1) * P], g_after[:, c, 4 * hh + hd, :], upto,
                                           start=False, stop=(hd == 3), skip_group_check=True)
                        mm.then_inc(pe_gdn.sem, pe_gdn.mark(what))
                pe.matmul(misc[:, 32:40], after, g_tok[:, 0, :], start=True, stop=True)
                pe.matmul(misc[:, 40:48], upto, g_tok[:, 1, :], start=True, stop=True)\
                    .then_inc(pe_gdn.sem, pe_gdn.mark("g_sums"))

                def squares(j):
                    pe.wait_ge(*act_conv.at(layer, ("sq", j)))
                    for b in range(2):
                        for c in range(TILES):
                            mm = pe.matmul(misc[:, 16 * c + 2 * j + b:16 * c + 2 * j + b + 1],
                                           sq[:, j % 2, b * S + c * P:b * S + (c + 1) * P], one, start=True, stop=True)
                    mm.then_inc(pe_gdn.sem, pe_gdn.mark(("squares", j)))

                for i in range(4):
                    wide(("bk", i), h, (dve_conv, ("tap", 0, i)))
                    if i == 2:
                        pe.wait_ge(*act_gdn.at(layer, "e_cum"))
                    if i >= 2:
                        squares(i - 2)
                for c in range(TILES):
                    pe.wait_ge(*dve_idx.at(layer, ("bias", c)))
                    pe.wait_ge(*dve_rope.at(layer, ("q", 3)))
                    keys, n_h = (c + 1) * P, 4 // (c + 1)
                    for j in range(HEADS // n_h):
                        what = ("scores", c, j)
                        o = claim(what, (act_att, what))
                        for i in range(n_h):
                            hd = n_h * j + i
                            pe.matmul(o[:, i * keys:(i + 1) * keys], q[:, hd, c * P:(c + 1) * P],
                                      kT[:, hd // (HEADS // KV_HEADS), 0:keys], start=True, stop=False, skip_group_check=True)
                            mm = pe.matmul(o[:, i * keys:(i + 1) * keys], ident_b, sel_bias[:, c, 0:keys],
                                           start=False, stop=True, skip_group_check=True)
                        mm.then_inc(pe_att.sem, pe_att.mark(what))
                for i in range(4):
                    wide(("bq", i), h, (dve_conv, ("tap", 0, 4 + i)))
                    squares(2 + i)
                for j in range(HEADS // 2):
                    what = ("pt0", j)
                    o = claim(what, (act_att, what))
                    pe.wait_ge(*dve_att.at(layer, ("p", 0, j // 2)))
                    pe.wait_ge(*dve_att.at(layer, ("p", 1, j)))
                    for i in range(2):
                        pe.transpose(o[:, i * S:i * S + P], p0[:, 2 * j + i, :], ident)
                        tr = pe.transpose(o[:, i * S + P:(i + 1) * S], p1[:, 2 * j + i, 0:P], ident)
                    tr.then_inc(pe_att.sem, pe_att.mark(what))
                for j in range(HEADS // 4):
                    what = ("pt1", j)
                    o = claim(what, (act_att, what))
                    for i in range(4):
                        tr = pe.transpose(o[:, i * P:(i + 1) * P], p1[:, 4 * j + i, P:S], ident)
                    tr.then_inc(pe_att.sem, pe_att.mark(what))
                for i in range(4):
                    wide(("bv", i), h, (dve_conv, ("tap", 0, 8 + i)))
                    if i < 2:
                        squares(6 + i)

                for g in range(4):
                    c, hh = g // 2, g % 2
                    if g == 0:
                        pe.wait_ge(*dve_conv.at(layer, ("silu", 7)))
                    for kind, other in (("kk", 0), ("kq", 8)):
                        what = (kind, g)
                        o = claim(what, (dve_gdn, what))
                        for i in range(4):
                            hd = 4 * hh + i
                            mm = pe.matmul(o[:, i * P:(i + 1) * P], conv[:, hd, c * P:(c + 1) * P],
                                           conv[:, other + hd, c * P:(c + 1) * P], start=True, stop=True)
                        mm.then_inc(pe_gdn.sem, pe_gdn.mark(what))
                    wide(("ga", g), h, (act_gate, ("ga", g)))
                pe.wait_ge(*act_att.at(layer, ("pt1", 1)))
                pe.wait_ge(*act_copy.at(layer, "v"))
                for j in range(HEADS // 2):
                    what = ("att", j)
                    grp_kv = 2 * j // (HEADS // KV_HEADS)
                    o = claim(what, (dve_att, what))
                    pe.matmul(o, v_tok[:, 0, grp_kv * DH:(grp_kv + 1) * DH], pt0[:, 2 * j:2 * j + 2, :],
                              start=True, stop=False, skip_group_check=True)
                    o2 = o.rearrange("p (h t) -> p h t", h=2)
                    mm = pe.matmul(o2[:, :, P:S], v_tok[:, 1, grp_kv * DH:(grp_kv + 1) * DH], pt1[:, 2 * j:2 * j + 2, :],
                                   start=False, stop=True, skip_group_check=True)
                    mm.then_inc(pe_att.sem, pe_att.mark(what))
                for g in range(4):
                    wide(("gb", g), h, (act_gate, ("gb", g)))
                    c, hh = g // 2, g % 2
                    what = ("v_tok", g)
                    o = claim(what, (dve_gdn, what))
                    if g == 0:
                        pe.wait_ge(*dve_conv.at(layer, ("silu", 11)))
                    for i in range(4):
                        tr = pe.transpose(o[:, i * P:(i + 1) * P], conv[:, 16 + 4 * hh + i, c * P:(c + 1) * P], ident)
                    tr.then_inc(pe_gdn.sem, pe_gdn.mark(what))
                for hh in range(2):
                    what = ("k_tok", hh)
                    o = claim(what, (dve_gdn, what))
                    for i in range(4):
                        tr = pe.transpose(o[:, i * P:(i + 1) * P], conv[:, 4 * hh + i, 0:P], ident)
                    tr.then_inc(pe_gdn.sem, pe_gdn.mark(what))
                for g in range(4):
                    what = ("t_low", 1, g)
                    o = claim(what, (act_gdn, what))
                    pe.wait_ge(*dve_gdn.at(layer, ("t_up", g)))
                    for i in range(4):
                        tr = pe.transpose(o[:, i * P:(i + 1) * P], t_up[:, g, i, :], ident)
                    tr.then_inc(pe_gdn.sem, pe_gdn.mark(what))
                for s in LEVELS:
                    for g in range(4):
                        what = ("mt", s, g)
                        o = claim(what, (dve_gdn, what))
                        if s == LEVELS[0]:
                            pe.wait_ge(*act_gdn.at(layer, ("t_low", 1, g)))
                        else:
                            pe.wait_ge(*dve_gdn.at(layer, ("t_low", s // 2, g)))
                        for i in range(4):
                            mm = pe.matmul(o[:, i * 64:(i + 1) * 64], m_up[:, g, i, :], even(t_low[:, g, i:i + 1, :], s),
                                           start=True, stop=True)
                        mm.then_inc(pe_gdn.sem, pe_gdn.mark(what))
                    for g in range(4):
                        what = ("tmt", s, g)
                        o = claim(what, (dve_gdn, ("t_low", s, g)))
                        pe.wait_ge(*dve_gdn.at(layer, ("mt", s, g)))
                        if s != LEVELS[0]:
                            pe.wait_ge(*act_gdn.at(layer, ("t_up", s // 2, g)))
                        for i in range(4):
                            mm = pe.matmul(o[:, i * 64:(i + 1) * 64], t_up[:, g, i, :], prod[:, g, i, :], start=True, stop=True)
                        mm.then_inc(pe_gdn.sem, pe_gdn.mark(what))
                    for g in range(4):
                        what = ("t_up", s, g)
                        o = claim(what, (act_gdn, what))
                        pe.wait_ge(*dve_gdn.at(layer, ("t_low", s, g)))
                        for i in range(4):
                            tr = pe.transpose(o[:, i * P:(i + 1) * P], t_low[:, g, i, :], ident)
                        tr.then_inc(pe_gdn.sem, pe_gdn.mark(what))

                def solve(g):
                    what = ("solved", g)
                    o = claim(what, (dve_gdn, ("v_new", g)))
                    pe.wait_ge(*act_gdn.at(layer, ("t_up", LEVELS[-1], g)))
                    pe.wait_ge(*dve_gdn.at(layer, ("v_tok" if g < 2 else "rhs", g)))
                    for i in range(4):
                        mm = pe.matmul(o[:, i * P:(i + 1) * P], t_up[:, g, i, :], rhs[:, g, i, :], start=True, stop=True)
                    mm.then_inc(pe_gdn.sem, pe_gdn.mark(what))

                def read_out(g):
                    what = ("o", g)
                    o = claim(what, (act_gdn, ("o", g)))
                    for i in range(4):
                        mm = pe.matmul(o[:, i * P:(i + 1) * P], attn[:, g, i, :], v_new[:, g, i, :], start=True, stop=True)
                    mm.then_inc(pe_gdn.sem, pe_gdn.mark(what))

                for g in range(2):
                    solve(g)
                for g in range(2):
                    what = ("state", g)
                    o = claim(what, (act_gdn, what))
                    pe.wait_ge(*dve_gdn.at(layer, ("v_new", g)))
                    pe.wait_ge(*dve_gdn.at(layer, ("k_tok", g)))
                    for i in range(4):
                        mm = pe.matmul(o[:, i * P:(i + 1) * P], k_dec[:, 4 * g + i, :], v_new[:, g, i, :], start=True, stop=True)
                    mm.then_inc(pe_gdn.sem, pe_gdn.mark(what))
                for g in range(2):
                    what = ("ks", g)
                    o = claim(what, (dve_gdn, what))
                    pe.wait_ge(*act_gdn.at(layer, ("state", g)))
                    for i in range(4):
                        hd = 4 * g + i
                        mm = pe.matmul(o[:, i * P:(i + 1) * P], conv[:, hd, P:S], state[:, hd, :], start=True, stop=True)
                    mm.then_inc(pe_gdn.sem, pe_gdn.mark(what))
                for g in range(2):
                    read_out(g)
                for g in range(2):
                    what = ("qs", g)
                    o = claim(what, (dve_gdn, what))
                    for i in range(4):
                        hd = 4 * g + i
                        mm = pe.matmul(o[:, i * P:(i + 1) * P], conv[:, 8 + hd, P:S], state[:, hd, :], start=True, stop=True)
                    mm.then_inc(pe_gdn.sem, pe_gdn.mark(what))
                for g in range(2, 4):
                    solve(g)
                for g in range(2, 4):
                    pe.wait_ge(*dve_gdn.at(layer, ("v_new", g)))
                    read_out(g)
                for j in range(G_HEADS // 2):
                    what = ("yb", j)
                    o = claim(what, (dve_gdn, what))
                    if j == 0:
                        for g in range(4):
                            pe.wait_ge(*dve_gdn.at(layer, ("o_norm", g)))
                    for i in range(2):
                        hd = 2 * j + i
                        for c in range(TILES):
                            tr = pe.transpose(o[:, i * S + c * P:i * S + (c + 1) * P], o_tok[:, 2 * c + hd // 4, hd % 4, :], ident)
                    tr.then_inc(pe_gdn.sem, pe_gdn.mark(what))
                pe.wait_ge(*dve_gdn.at(layer, ("y", 3)))
                y_banks = lambda part: [[claim((part, c, half), (dve_norm, ("scaled", part, c)), (4 + 2 * c + half,))
                                         for half in range(2)] for c in range(TILES)]
                halves("out", y, y_banks("out"))
                xv = [[claim(("xv", c, half), (act_copy, ("xv", c, half)), range(4)) for half in range(2)] for c in range(TILES)]
                halves("xv", mem_gain, xv)
                norm_transposes("x")
                pe.wait_ge(*dve_norm.at(layer, ("h", "x", 1, 1)))
                for i in range(4):
                    wide(("xq", i), h, (act_copy, ("xq", i)), range(4))
                for c in range(TILES):
                    for j in range(2):
                        what = ("xs", c, j)
                        o = claim(what, (act_att, what))
                        pe.wait_ge(*act_copy.at(layer, ("xq", 2 * j + 1)))
                        for i in range(2):
                            hd = 2 * j + i
                            for b in range(2):
                                mm = pe.matmul(o[:, i * S:(i + 1) * S], qx[:, 2 * hd + b, c * P:(c + 1) * P], kx[:, 2 * hd + b, :],
                                               start=(b == 0), stop=(b == 1))
                        mm.then_inc(pe_x.sem, pe_x.mark(what))
                for j in range(2):
                    for b in range(2):
                        what = ("xpt", b, j)
                        o = claim(what, (act_att, what))
                        for c in range(TILES):
                            pe.wait_ge(*dve_att.at(layer, ("px", c, j)))
                        for i in range(2):
                            for c in range(TILES):
                                tr = pe.transpose(o[:, i * S + c * P:i * S + (c + 1) * P], px[:, c, 2 * j + i, b * P:(b + 1) * P], ident)
                        tr.then_inc(pe_x.sem, pe_x.mark(what))
                for j in range(4):
                    what = ("ox", j)
                    o = claim(what, (act_att, what))
                    pe.wait_ge(*act_att.at(layer, ("xpt", 1, j // 2)))
                    for i in range(2):
                        for b in range(2):
                            mm = pe.matmul(o[:, i * S:(i + 1) * S], vx[:, b, (2 * j + i) * P:(2 * j + i + 1) * P], pxt[:, b, j, :],
                                           start=(b == 0), stop=(b == 1))
                    mm.then_inc(pe_x.sem, pe_x.mark(what))
                pe.wait_ge(*act_att.at(layer, ("ox", 3)))
                halves("xo", ox, y_banks("xo"))
                norm_transposes("ffn")
                pe.wait_ge(*dve_norm.at(layer, ("h", "ffn", 1, 1)))
                for i in range(FF // 256):
                    wide(("gate", i), h, (dve_ff, ("silu", i)), range(4))
                    wide(("up", i), h, (dve_ff, ("ff", i)), range(4))
                down = y_banks("down")
                for i in range(FF_BLOCKS // 2):
                    w = weights_here(SLOT_AT["down", i]).rearrange("p (k n) -> p k n", k=2)
                    pe.wait_ge(*dve_ff.at(layer, ("ff", i)))
                    for c in range(TILES):
                        for k in range(2):
                            for half in range(2):
                                mm = pe.matmul(down[c][half], ff[:, 2 * i + k, c * P:(c + 1) * P], w[:, k, half * 512:(half + 1) * 512],
                                               start=(i == 0 and k == 0), stop=(i == FF_BLOCKS // 2 - 1 and k == 1))
                        if c == 0 and i == FF_BLOCKS // 2 - 1:
                            mm.then_inc(pe_out.sem, pe_out.mark("down"))
                    mm.then_inc(slots.sem, slots.mark(("down", i)))

        @block.scalar
        def _(act):
            act.dma_start(param_t[:, :], params[0]).then_inc(param_loaded, 16)
            act.dma_start(gain_t[:, :], post_gains[0:1, :].broadcast_to([P, D])).then_inc(gain_loaded, 16)
            act.wait_ge(mem_loaded, 16)
            for c in range(TILES):
                nc.scalar.activation(xn[:, c, :], mem_block(kx_t)[:, c, :], ACT.Square, scale=D ** -0.5, accum_out=ss[:, c:c + 1]).then_inc(mem_act, 1)
            for w in range(4):
                act.wait_ge(*table.at(0, ("angle", w)))
                nc.scalar.activation(rope[:, w, :], angle(w), ACT.Sin).then_inc(tables_act, 1)
            act.wait_ge(mem_pool, 2 * TILES)
            act.wait_ge(mem_act, TILES)

            with act.Fori(0, DEPTH) as layer:
                def square_x(which, c):
                    nc.scalar.activation(xn[:, c, :], x[:, c, :], ACT.Square, scale=D ** -0.5, accum_out=ss[:, c:c + 1])\
                        .then_inc(act_norm.sem, act_norm.mark(("ss", which, c)))

                def post_and_pre_norm(part, product, row, which):
                    for c in range(TILES):
                        if c == 0:
                            act.wait_ge(*pe_out.at(layer, product))
                        else:
                            act.wait_ge(*slots.at(layer, (product, LAST[product])))
                        nc.scalar.activation(xn[:, c, :], y_tile(c), ACT.Square, scale=D ** -0.5, accum_out=ss2[:, c:c + 1])\
                            .then_inc(act_norm.sem, act_norm.mark(("ss2", part, c)))
                    if which is not None:
                        for c in range(TILES):
                            act.wait_ge(*dve_norm.at(layer, ("x", part, c)))
                            square_x(which, c)
                    act.wait_ge(*dve_norm.at(layer, ("scaled", part, 1)))
                    act.dma_start(gain_t[:, :], post_gains[bass.ds(layer * 3 + row, 1), :].broadcast_to([P, D]))\
                        .then_inc(gain_loaded, 16)

                def copy(out, src, producer, what, done, name, **kw):
                    act.wait_ge(*producer.at(layer, what))
                    nc.scalar.activation(out, src, ACT.Copy, **kw).then_inc(done.sem, done.mark(name))

                for c in range(TILES):
                    act.wait_ge(x_ready, layer * TILES + c + 1)
                    square_x("mix", c)
                for i in range(4):
                    copy(flat(kx[:, 2 * i:2 * i + 2, :]), bank(("xk", i)), slots, ("xk", i), act_copy, ("xk", i))
                act.wait_ge(*dve_rope.at(layer, ("cos", "ik")))
                copy(small, bank(("small", 0))[:, S:S + 40].rearrange("p (c n) -> p c n", c=TILES), slots, ("small", 0), act_copy, "small")
                act.wait_ge(*act_copy.at(layer, "small"))
                nc.scalar.activation(beta, small[:, :, 12:20], ACT.Tanh, scale=0.5).then_inc(act_gdn.sem, act_gdn.mark("beta"))
                nc.scalar.activation(a_exp, param_t[:, R_ALOG:R_ALOG + 8], ACT.Exp).then_inc(act_gdn.sem, act_gdn.mark("a"))
                act.wait_ge(*dve_gate.at(layer, "abs"))
                nc.scalar.activation(ga_e, ga_abs, ACT.Exp, scale=-1.0).then_inc(act_gdn.sem, act_gdn.mark("e"))
                act.wait_ge(*dve_gate.at(layer, "w"))
                nc.scalar.activation(ga_ln, ga_w, ACT.Ln).then_inc(act_gdn.sem, act_gdn.mark("ln"))
                copy(flat(v_tok), bank(("v", 0)), slots, ("v", 0), act_copy, "v", scale=0.5)
                for c in range(TILES):
                    keys = (c + 1) * P
                    if c == 1:
                        act.wait_ge(*dve_idx.at(layer, ("score", 0)))
                    for odd in range(2):
                        what = ("logits", c, odd)
                        act.wait_ge(*pe_idx.at(layer, what))
                        nc.scalar.activation(idx_relu[:, odd:odd + 3:2, 0:keys],
                                             bank(what)[:, 0:2 * keys].rearrange("p (h s) -> p h s", h=2), ACT.Relu)\
                            .then_inc(act_att.sem, act_att.mark(what))
                for c in range(TILES):
                    for hh in range(2):
                        what = ("decay", c, hh)
                        act.wait_ge(*pe_gdn.at(layer, what))
                        nc.scalar.activation(flat(decay[:, 2 * c + hh, :, :]), bank(what), ACT.Exp).then_inc(act_gdn.sem, act_gdn.mark(what))
                act.wait_ge(*pe_gdn.at(layer, "g_sums"))
                nc.scalar.activation(e_last, psum[:, 7, 32:40], ACT.Exp).then_inc(act_gdn.sem, act_gdn.mark("e_last"))
                nc.scalar.activation(e_cum, psum[:, 7, 40:48], ACT.Exp).then_inc(act_gdn.sem, act_gdn.mark("e_cum"))

                def conv_last_tap(j):
                    key = CONV_SLOTS[j]
                    act.wait_ge(*slots.at(layer, key))
                    for b in range(2):
                        nc.scalar.activation(conv[:, 2 * j + b, :], bank(key)[:, b * S:(b + 1) * S], ACT.Copy,
                                             scale=tap(3, 2 * j + b)).then_inc(act_conv.sem, act_conv.mark(("conv", j, b)))

                def conv_tanh(j):
                    act.wait_ge(*dve_conv.at(layer, ("tap", 0, j)))
                    if j >= 2:
                        act.wait_ge(*dve_conv.at(layer, ("silu", j - 2)))
                    nc.scalar.activation(th[:, j % 2, :], flat(conv[:, 2 * j:2 * j + 2, :]), ACT.Tanh, scale=0.5)\
                        .then_inc(act_conv.sem, act_conv.mark(("tanh", j)))

                def conv_square(j):
                    act.wait_ge(*dve_conv.at(layer, ("silu", j)))
                    if j >= 2:
                        act.wait_ge(*pe_gdn.at(layer, ("squares", j - 2)))
                    nc.scalar.activation(sq[:, j % 2, :], flat(conv[:, 2 * j:2 * j + 2, :]), ACT.Square)\
                        .then_inc(act_conv.sem, act_conv.mark(("sq", j)))

                def conv_step(j):
                    if j < 12:
                        conv_last_tap(j)
                    if 1 <= j <= 12:
                        conv_tanh(j - 1)
                    if 2 <= j < 10:
                        conv_square(j - 2)

                for j in range(4):
                    conv_step(j)
                for c in range(TILES):
                    keys, n_h = (c + 1) * P, 4 // (c + 1)
                    for j in range(HEADS // n_h):
                        act.wait_ge(*dve_att.at(layer, ("max", c, j)))
                        for i in range(n_h):
                            hd = n_h * j + i
                            ins = nc.scalar.activation((p0, p1)[c][:, hd, :], bank(("scores", c, j))[:, i * keys:(i + 1) * keys], ACT.Exp,
                                                       bias=nmx[:, c, hd:hd + 1], scale=DH ** -0.5, accum_out=psumr[:, c, hd:hd + 1])
                        ins.then_inc(act_att.sem, act_att.mark(("scores", c, j)))
                for j in range(4, 8):
                    conv_step(j)
                for j in range(HEADS // 2):
                    copy(flat(pt0[:, 2 * j:2 * j + 2, :]), bank(("pt0", j)), pe_att, ("pt0", j), act_att, ("pt0", j))
                for j in range(HEADS // 4):
                    copy(flat(pt1[:, 4 * j:4 * j + 4, :]), bank(("pt1", j)), pe_att, ("pt1", j), act_att, ("pt1", j))
                for j in range(8, 13):
                    conv_step(j)

                def gate(part, i, block0):
                    act.wait_ge(*slots.at(layer, (part, i)))
                    nc.scalar.activation(flat(gates[:, block0 + 2 * i:block0 + 2 * i + 2, :]), bank((part, i)), ACT.Tanh, scale=0.5)\
                        .then_inc(act_gate.sem, act_gate.mark((part, i)))

                for i in range(4):
                    gate("ga", i, 0)
                for i in range(4):
                    gate("gb", i, 8)
                for g in range(4):
                    copy(flat(t_low[:, g, :, :]), bank(("t_low", 1, g)), pe_gdn, ("t_low", 1, g), act_gdn, ("t_low", 1, g))
                for s in LEVELS:
                    for g in range(4):
                        copy(flat(t_up[:, g, :, :]), bank(("t_up", s, g)), pe_gdn, ("t_up", s, g), act_gdn, ("t_up", s, g))
                for g in range(2):
                    copy(flat(state[:, 4 * g:4 * g + 4, :]), bank(("state", g)), pe_gdn, ("state", g), act_gdn, ("state", g))
                for g in range(4):
                    copy(flat(o_tok[:, g, :, :]), bank(("o", g)), pe_gdn, ("o", g), act_gdn, ("o", g))
                    if g >= 2:
                        act.wait_ge(*dve_gdn.at(layer, ("o", g)))
                        act.wait_ge(*dve_gdn.at(layer, ("oss", g - 2)))
                    else:
                        act.wait_ge(*act_gdn.at(layer, ("o", g)))
                        act.wait_ge(*dve_gdn.at(layer, ("rhs", 2 + g)))
                    nc.scalar.activation(th[:, g % 2, :], flat(o_tok[:, g, :, :]), ACT.Square).then_inc(act_gdn.sem, act_gdn.mark(("o_sq", g)))
                post_and_pre_norm("mix", "out", 1, "x")
                for c in range(TILES):
                    for half in range(2):
                        copy(vx[:, c, half * 512:(half + 1) * 512], bank(("xv", c, half)), slots, ("xv", 3), act_copy, ("xv", c, half))
                for i in range(4):
                    copy(flat(qx[:, 2 * i:2 * i + 2, :]), bank(("xq", i)), slots, ("xq", i), act_copy, ("xq", i))
                for c in range(TILES):
                    for j in range(2):
                        act.wait_ge(*dve_att.at(layer, ("xmax", c, j)))
                        for i in range(2):
                            hd = 2 * j + i
                            ins = nc.scalar.activation(px[:, c, hd, :], bank(("xs", c, j))[:, i * S:(i + 1) * S], ACT.Exp,
                                                       bias=nmx[:, c, hd:hd + 1], scale=X_DH ** -0.5, accum_out=psumr[:, c, hd:hd + 1])
                        ins.then_inc(act_att.sem, act_att.mark(("xs", c, j)))
                for j in range(2):
                    for b in range(2):
                        copy(flat(pxt[:, b, 2 * j:2 * j + 2, :]), bank(("xpt", b, j)), pe_x, ("xpt", b, j), act_att, ("xpt", b, j))
                for j in range(4):
                    copy(flat(ox[:, 2 * j:2 * j + 2, :]), bank(("ox", j)), pe_x, ("ox", j), act_att, ("ox", j))
                post_and_pre_norm("x", "xo", 2, "ffn")
                act.wait_ge(*dve_norm.at(layer, ("h", "ffn", 1, 1)))
                act.dma_start(param_t[:, :], params[bass.ds(layer + 1, 1), :, :].rearrange("a p n -> p (a n)")).then_inc(param_loaded, 16)
                for i in range(FF // 256):
                    act.wait_ge(*slots.at(layer, ("gate", i)))
                    if i >= 2:
                        act.wait_ge(*dve_ff.at(layer, ("silu", i - 2)))
                    nc.scalar.activation(th[:, i % 2, :], bank(("gate", i)), ACT.Tanh, scale=0.5).then_inc(act_ff.sem, act_ff.mark(("tanh", i)))
                post_and_pre_norm("ffn", "down", 3, None)
            act.wait_ge(param_loaded, 16 * (DEPTH + 1))
            act.wait_ge(gain_loaded, 16 * (3 * DEPTH + 1))

        @block.gpsimd
        def _(pool):
            pool.wait_ge(consts_loaded, 32)
            for c in range(TILES):
                pool.wait_ge(mem_act, c + 1)
                nc.gpsimd.tensor_tensor(rs[:, c:c + 1], ss[:, c:c + 1], eps_col, ALU.add).then_inc(mem_pool, 1)
                pool.wait_ge(mem_pool, 2 * c + 1)
                nc.gpsimd.tensor_tensor(rs[:, c:c + 1], rs[:, c:c + 1], neghalf[:, 0:1], ALU.pow).then_inc(mem_pool, 1)

            def apply_mem_gain():
                nc.gpsimd.tensor_tensor(mem_gain, mem_feat, cols(param_t[:, R_MEM:R_MEM + KT], S), ALU.mult)\
                    .then_inc(mem_gain_ready, 1)

            pool.wait_ge(param_loaded, 16)
            pool.wait_ge(mem_dve, 3 * TILES)
            apply_mem_gain()
            with pool.Fori(0, DEPTH) as layer:
                def rsqrt(sums, r, ready, what, name):
                    pool.wait_ge(*ready.at(layer, what))
                    nc.gpsimd.tensor_tensor(r, sums, eps_col, ALU.add).then_inc(pool_norm.sem, pool_norm.mark(("mean", name)))
                    pool.wait_ge(*pool_norm.at(layer, ("mean", name)))
                    nc.gpsimd.tensor_tensor(r, r, neghalf[:, 0:1], ALU.pow).then_inc(pool_norm.sem, pool_norm.mark(name))

                def prenorm(which):
                    for c in range(TILES):
                        rsqrt(ss[:, c:c + 1], rs[:, c:c + 1], act_norm, ("ss", which, c), ("pre", which, c))

                def postnorm(part):
                    for c in range(TILES):
                        rsqrt(ss2[:, c:c + 1], rs2[:, c:c + 1], act_norm, ("ss2", part, c), ("post", part, c))

                prenorm("mix")
                pool.wait_ge(*dve_gdn.at(layer, "ss"))
                nc.gpsimd.tensor_tensor(rk, ss_kq[:, :, 0:8], neghalf.rearrange("p (c h) -> p c h", c=TILES), ALU.pow)\
                    .then_inc(pool_gdn.sem, pool_gdn.mark("rk"))
                for g in range(4):
                    c, hh = g // 2, g % 2
                    o = oscale[:, c, 4 * hh:4 * hh + 4]
                    pool.wait_ge(*dve_gdn.at(layer, ("o_mean", g)))
                    nc.gpsimd.tensor_tensor(o, o, neghalf[:, 0:4], ALU.pow).then_inc(pool_gdn.sem, pool_gdn.mark(("o_scale", g)))
                postnorm("mix")
                prenorm("x")
                postnorm("x")
                prenorm("ffn")
                pool.wait_ge(param_loaded, 16 * (layer + 2))
                pool.wait_ge(*slots.at(layer, ("xv", 3)))
                apply_mem_gain()
                postnorm("ffn")

        @block.vector
        def _(dve):
            dve.wait_ge(consts_loaded, 32)
            dve.wait_ge(pos_loaded, 16)
            pos = y_t[:, S:2 * S]
            nc.vector.tensor_copy(pos, y_t[:, 0:S].bitcast(I32)).then_inc(table.sem, table.mark("pos"))
            dve.wait_ge(*table.at(0, "pos"))
            ang, turns = rb_t[:, 0:S], rb_t[:, S:2 * S]
            for w, inv, sgn in ((0, C_INV_A, C_SGN_A), (2, C_INV_I, C_SGN_I)):
                r = angle(w + 1)

                def then(ins, name):
                    ins.then_inc(table.sem, table.mark((name, w)))
                    dve.wait_ge(*table.at(0, (name, w)))

                then(nc.vector.tensor_scalar(ang, pos, const_t[:, inv:inv + 1], None, ALU.mult), "ang")
                then(nc.vector.tensor_scalar(turns, ang, 1 / (2 * PI), ROUND, ALU.mult, ALU.add), "round")
                then(nc.vector.tensor_scalar(turns, turns, ROUND, None, ALU.subtract), "turns")
                for n, part in enumerate((TWO_PI_1, TWO_PI_2, TWO_PI_3)):
                    then(nc.vector.scalar_tensor_tensor(out=ang, in0=turns, scalar=-part, in1=ang, op0=ALU.mult, op1=ALU.add), f"less{n}")
                then(nc.vector.tensor_scalar(ang, ang, PI_BELOW, -PI_BELOW, ALU.min, ALU.max), "clamp")
                nc.vector.tensor_scalar(r, ang, const_t[:, sgn:sgn + 1], None, ALU.mult).then_inc(table.sem, table.mark(("angle", w + 1)))
                then(nc.vector.scalar_tensor_tensor(out=turns, in0=ang, scalar=-1.0, in1=ang, op0=ALU.mult, op1=ALU.max), "abs")
                nc.vector.tensor_scalar(angle(w), turns, -1.0, PI / 2, ALU.mult, ALU.add).then_inc(table.sem, table.mark(("angle", w)))
                dve.wait_ge(*table.at(0, ("angle", w)))
            for c in range(TILES):
                m = mem_block(kx_t)[:, c, :]
                dve.wait_ge(mem_pool, 2 * c + 2)
                nc.vector.tensor_scalar(m, m, rs[:, c:c + 1], None, ALU.mult).then_inc(mem_dve, 1)
            for j in range(4):
                c, half = j // 2, j % 2
                dve.wait_ge(mem_pe, j + 1)
                nc.vector.tensor_copy(mem_feat[:, 4 * half:4 * half + 4, c * P:(c + 1) * P],
                                      psum[:, j, :].rearrange("p (k t) -> p k t", k=4)).then_inc(mem_dve, 1)
            dve.wait_ge(x_loaded, 16)
            dve.wait_ge(tables_act, 4)
            for c in range(TILES):
                nc.vector.memset(top8[:, c:c + 1], 0.0).then_inc(x_ready, 1)
            dve.wait_ge(x_ready, TILES)

            with dve.Fori(0, DEPTH) as layer:
                V = nc.vector

                def link(ins, done, name):
                    ins.then_inc(done.sem, done.mark(name))
                    dve.wait_ge(*done.at(layer, name))

                def prenorm(which, gain):
                    for c in range(TILES):
                        dve.wait_ge(*pool_norm.at(layer, ("pre", which, c)))
                        V.tensor_scalar(xn[:, c, :], x[:, c, :], rs[:, c:c + 1], None, ALU.mult)\
                            .then_inc(dve_norm.sem, dve_norm.mark(("xn", which, c)))
                    for c in range(TILES):
                        for half in range(2):
                            what = ("h", which, c, half)
                            dve.wait_ge(*pe_t.at(layer, what))
                            V.tensor_tensor(h[:, 4 * half:4 * half + 4, c * P:(c + 1) * P],
                                            bank(what).rearrange("p (k t) -> p k t", k=4),
                                            cols(param_t[:, gain + 4 * half:gain + 4 * half + 4], P), ALU.mult)\
                                .then_inc(dve_norm.sem, dve_norm.mark(what))

                def postnorm(part, row, final=False):
                    dve.wait_ge(gain_loaded, 16 * (3 * layer + row + 1))
                    for c in range(TILES):
                        dve.wait_ge(*pool_norm.at(layer, ("post", part, c)))
                        link(V.scalar_tensor_tensor(out=xn[:, c, :], in0=y_tile(c), scalar=rs2[:, c:c + 1], in1=gain_t[:, :],
                                                    op0=ALU.mult, op1=ALU.mult), dve_norm, ("scaled", part, c))
                        ins = V.tensor_tensor(x[:, c, :], x[:, c, :], xn[:, c, :], ALU.add)
                        if final:
                            ins.then_inc(x_ready, 1)
                        else:
                            ins.then_inc(dve_norm.sem, dve_norm.mark(("x", part, c)))

                def rotate(what, key, out, blocks, cos, half, name, buf):
                    src = bank(key)[:, 0:blocks * S].rearrange("p (b t) -> p b t", b=blocks)
                    tmp = rope_tmp[:, buf, 0:blocks * S].rearrange("p (b t) -> p b t", b=blocks)
                    dve.wait_ge(*slots.at(layer, key))
                    for lo in range(0, P, half):
                        o = lo ^ half
                        V.tensor_tensor(tmp[lo:lo + half], src[o:o + half],
                                        rope[o:o + half, cos + 1, :].unsqueeze(1).broadcast_to([half, blocks, S]), ALU.mult)\
                            .then_inc(dve_rope.sem, dve_rope.mark(("partner", name, lo)))
                    link(V.tensor_tensor(out, src, heads(rope[:, cos, :], blocks), ALU.mult), dve_rope, ("cos", name))
                    link(V.tensor_tensor(out, out, tmp, ALU.add), dve_rope, name)

                prenorm("mix", R_MIX)
                rotate("iq", ("iq", 0), iq, 2, 2, 32, "iq", 0)
                rotate("ik", ("small", 0), ik.unsqueeze(1), 1, 2, 32, "ik", 1)
                dve.wait_ge(*act_copy.at(layer, "small"))
                link(V.tensor_tensor(ga_x, small[:, :, 4:12], heads(param_t[:, R_DT:R_DT + 8], TILES), ALU.add), dve_gate, "x")
                link(V.scalar_tensor_tensor(out=ga_abs, in0=ga_x, scalar=-1.0, in1=ga_x, op0=ALU.mult, op1=ALU.max), dve_gate, "abs")
                dve.wait_ge(*act_gdn.at(layer, "e"))
                link(V.tensor_scalar(ga_w, ga_e, 1.0, None, ALU.add), dve_gate, "w")
                link(V.scalar_tensor_tensor(out=ga_t, in0=ga_w, scalar=-1.0, in1=ga_e, op0=ALU.add, op1=ALU.subtract), dve_gate, "t")
                link(V.reciprocal(ga_r, ga_w), dve_gate, "r")
                link(V.tensor_tensor(ga_t, ga_t, ga_r, ALU.mult), dve_gate, "t2")
                dve.wait_ge(*act_gdn.at(layer, "ln"))
                link(V.tensor_tensor(ga_t, ga_ln, ga_t, ALU.subtract), dve_gate, "log1p")
                link(V.scalar_tensor_tensor(out=ga_t, in0=ga_x, scalar=0.0, in1=ga_t, op0=ALU.max, op1=ALU.add), dve_gate, "softplus")
                link(V.scalar_tensor_tensor(out=g_tok, in0=ga_t, scalar=-1.0, in1=heads(a_exp, TILES), op0=ALU.mult, op1=ALU.mult), dve_gate, "g")
                link(V.tensor_scalar(beta, beta, 0.5, 0.5, ALU.mult, ALU.add), dve_gate, "beta")
                V.tensor_scalar(half_gdn, param_t[:, R_GDN:R_GDN + 1], 0.5, None, ALU.mult).then_inc(dve_gate.sem, dve_gate.mark("half_gdn"))
                for c in range(TILES):
                    V.tensor_tensor(g_after[:, c, :, :], heads(after, G_HEADS), cols(g_tok[:, c, :], P), ALU.mult)\
                        .then_inc(dve_gate.sem, dve_gate.mark(("g_after", c)))
                rotate("k", ("k", 0), kT, 2, 0, 64, "k", 0)
                rotate("q0", ("q", 0), q[:, 0:2, :], 2, 0, 64, ("q", 0), 1)
                for c in range(TILES):
                    keys = (c + 1) * P
                    val = idx_val[:, c, 0:keys]
                    diag = idx_val[:, c, c * P:(c + 1) * P]
                    dve.wait_ge(*act_att.at(layer, ("logits", c, 0)))
                    dve.wait_ge(*act_att.at(layer, ("logits", c, 1)))
                    link(V.tensor_scalar(val, idx_relu[:, 0, 0:keys], small[:, c, 0:1], None, ALU.mult), dve_idx, ("w0", c))
                    for hd in range(1, IDX_HEADS):
                        link(V.scalar_tensor_tensor(out=val, in0=idx_relu[:, hd, 0:keys], scalar=small[:, c, hd:hd + 1], in1=val,
                                                    op0=ALU.mult, op1=ALU.add), dve_idx, ("score", c) if hd == 3 else ("w", c, hd))
                    V.tensor_tensor(diag, diag, idx_bias, ALU.add)
                    for n in range(TOPK // 8):
                        dve.drain()
                        V.max(top8, val)
                        dve.drain()
                        V.match_replace(val, top8, val, TAKEN)
                    dve.drain()
                    link(V.tensor_scalar(sel_bias[:, c, 0:keys], val, TAKEN / 2, NEG, ALU.is_gt, ALU.mult), dve_idx, ("sel", c))
                    sel_diag = sel_bias[:, c, c * P:(c + 1) * P]
                    link(V.tensor_tensor(sel_diag, sel_diag, idx_bias, ALU.min), dve_idx, ("bias", c))
                for i in range(1, 4):
                    rotate("q", ("q", i), q[:, 2 * i:2 * i + 2, :], 2, 0, 64, ("q", i), (i + 1) % 2)

                def conv_taps(j):
                    for d in range(1, CONV_K):
                        for b in range(2):
                            blk = 2 * j + b
                            if d == 1:
                                dve.wait_ge(*act_conv.at(layer, ("conv", j, 1)))
                            else:
                                dve.wait_ge(*dve_conv.at(layer, ("tap" if b else "tap_a", 4 - d, j)))
                            V.scalar_tensor_tensor(out=conv[:, blk, d:S], in0=bank(CONV_SLOTS[j])[:, b * S:(b + 1) * S - d],
                                                   scalar=tap(3 - d, blk), in1=conv[:, blk, d:S], op0=ALU.mult, op1=ALU.add)\
                                .then_inc(dve_conv.sem, dve_conv.mark(("tap" if b else "tap_a", 3 - d, j)))

                def conv_silu(j):
                    c2 = flat(conv[:, 2 * j:2 * j + 2, :])
                    dve.wait_ge(*act_conv.at(layer, ("tanh", j)))
                    V.scalar_tensor_tensor(out=c2, in0=th[:, j % 2, :], scalar=1.0, in1=c2, op0=ALU.add, op1=ALU.mult)\
                        .then_inc(dve_conv.sem, dve_conv.mark(("silu", j)))

                def conv_step(j):
                    if j < 12:
                        conv_taps(j)
                    if j >= 1:
                        conv_silu(j - 1)

                def row_max(scores, c, h0, n_h, scale, name):
                    link(V.tensor_reduce(mx[:, c, h0:h0 + n_h], scores, AX_X, ALU.max), dve_att, ("mx", name))
                    V.tensor_scalar(nmx[:, c, h0:h0 + n_h], mx[:, c, h0:h0 + n_h], -scale, None, ALU.mult)\
                        .then_inc(dve_att.sem, dve_att.mark(name))

                def normalise(pr, c, h0, n_h, name):
                    link(V.reciprocal(pinv[:, c, h0:h0 + n_h], psumr[:, c, h0:h0 + n_h]), dve_att, ("inv", name))
                    V.tensor_tensor(pr, pr, cols(pinv[:, c, h0:h0 + n_h], pr.shape[-1]), ALU.mult)\
                        .then_inc(dve_att.sem, dve_att.mark(name))

                for j in range(4):
                    conv_step(j)
                for c in range(TILES):
                    keys, n_h = (c + 1) * P, 4 // (c + 1)
                    for j in range(HEADS // n_h):
                        dve.wait_ge(*pe_att.at(layer, ("scores", c, j)))
                        row_max(bank(("scores", c, j)).rearrange("p (h s) -> p h s", h=n_h), c, n_h * j, n_h, DH ** -0.5, ("max", c, j))
                for j in range(4, 6):
                    conv_step(j)
                for c in range(TILES):
                    n_h = 4 // (c + 1)
                    for j in range(HEADS // n_h):
                        dve.wait_ge(*act_att.at(layer, ("scores", c, j)))
                        normalise((p0, p1)[c][:, n_h * j:n_h * (j + 1), :], c, n_h * j, n_h, ("p", c, j))
                for j in range(6, 11):
                    conv_step(j)
                dve.wait_ge(*pe_gdn.at(layer, ("squares", 7)))
                link(V.tensor_scalar(ss_kq, psum[:, 7, 0:32].rearrange("p (c b) -> p c b", c=TILES), 4 * EPS, None, ALU.add), dve_gdn, "ss")
                for j in range(11, 13):
                    conv_step(j)
                V.tensor_scalar(o_eps, ss_kq[:, :, 8:16], DH * EPS, None, ALU.mult).then_inc(dve_gdn.sem, dve_gdn.mark("o_eps"))
                dve.wait_ge(*pool_gdn.at(layer, "rk"))
                dve.wait_ge(*act_gdn.at(layer, "e_last"))
                V.scalar_tensor_tensor(out=v_scale, in0=ss_kq[:, :, 0:8], scalar=0.5, in1=rk, op0=ALU.mult, op1=ALU.mult)\
                    .then_inc(dve_gdn.sem, dve_gdn.mark("v_scale"))
                V.tensor_tensor(k_scale0, rk[:, 0, :], e_last, ALU.mult).then_inc(dve_gdn.sem, dve_gdn.mark("k_scale0"))
                link(V.tensor_tensor(d_k, beta, rk, ALU.mult), dve_gdn, "d_k")
                link(V.tensor_tensor(m_scale, d_k, rk, ALU.mult), dve_gdn, "m_scale")
                for g in range(4):
                    c, hh = g // 2, g % 2
                    dve.wait_ge(*act_gdn.at(layer, ("decay", c, hh)))
                    for kind, dst, scale in (("kk", m_up, m_scale), ("kq", attn, rk)):
                        dve.wait_ge(*pe_gdn.at(layer, (kind, g)))
                        for i in range(4):
                            ins = V.scalar_tensor_tensor(out=dst[:, g, i, :], in0=bank((kind, g))[:, i * P:(i + 1) * P],
                                                         scalar=scale[:, c, 4 * hh + i:4 * hh + i + 1], in1=decay[:, g, i, :],
                                                         op0=ALU.mult, op1=ALU.mult)
                        ins.then_inc(dve_gdn.sem, dve_gdn.mark((kind, g)))
                    dve.wait_ge(*dve_gdn.at(layer, ("kk", g)))
                    link(V.tensor_tensor(t_up[:, g, :, :], m_up[:, g, :, :], heads(mask1, 4), ALU.mult), dve_gdn, ("m1", g))
                    V.scalar_tensor_tensor(out=t_up[:, g, :, :], in0=t_up[:, g, :, :], scalar=-1.0, in1=heads(ident, 4),
                                           op0=ALU.mult, op1=ALU.add).then_inc(dve_gdn.sem, dve_gdn.mark(("t_up", g)))
                for j in range(HEADS // 2):
                    dve.wait_ge(*act_gate.at(layer, ("ga", j)))
                    dve.wait_ge(*pe_att.at(layer, ("att", j)))
                    V.scalar_tensor_tensor(out=flat(y[:, 2 * j:2 * j + 2, :]), in0=flat(gates[:, 2 * j:2 * j + 2, :]), scalar=1.0,
                                           in1=bank(("att", j)), op0=ALU.add, op1=ALU.mult).then_inc(dve_att.sem, dve_att.mark(("att", j)))

                def by_head(out, what, scale, name):
                    dve.wait_ge(*pe_gdn.at(layer, what))
                    V.tensor_tensor(out, bank(what).rearrange("p (h n) -> p h n", h=4), cols(scale, P), ALU.mult)\
                        .then_inc(dve_gdn.sem, dve_gdn.mark(name))

                for g in range(4):
                    by_head(rhs[:, g, :, :], ("v_tok", g), v_scale[:, g // 2, 4 * (g % 2):4 * (g % 2) + 4], ("v_tok", g))
                for g in range(2):
                    by_head(k_dec[:, 4 * g:4 * g + 4, :], ("k_tok", g), k_scale0[:, 4 * g:4 * g + 4], ("k_tok", g))
                for n, s in enumerate(LEVELS):
                    level_mask = const_t[:, C_LEVEL + 64 * n:C_LEVEL + 64 * (n + 1)]
                    for g in range(4):
                        dve.wait_ge(*pe_gdn.at(layer, ("mt", s, g)))
                        V.tensor_tensor(prod[:, g, :, :], bank(("mt", s, g))[:, 0:256].rearrange("p (h n) -> p h n", h=4),
                                        heads(level_mask, 4), ALU.mult).then_inc(dve_gdn.sem, dve_gdn.mark(("mt", s, g)))
                    for g in range(4):
                        dve.wait_ge(*pe_gdn.at(layer, ("tmt", s, g)))
                        t = even(t_low[:, g, :, :], s)
                        V.tensor_tensor(t, t, bank(("tmt", s, g))[:, 0:256].rearrange("p (b c) -> p b c", c=s), ALU.subtract)\
                            .then_inc(dve_gdn.sem, dve_gdn.mark(("t_low", s, g)))
                for g in range(2):
                    by_head(v_new[:, g, :, :], ("solved", g), d_k[:, 0, 4 * g:4 * g + 4], ("v_new", g))
                for g in range(2):
                    pred = th[:, g, :].rearrange("p (h n) -> p h n", h=4)
                    by_head(pred, ("ks", g), e_cum[:, 4 * g:4 * g + 4], ("ks", g))
                    dve.wait_ge(*dve_gdn.at(layer, ("ks", g)))
                    V.tensor_tensor(rhs[:, 2 + g, :, :], rhs[:, 2 + g, :, :], pred, ALU.subtract).then_inc(dve_gdn.sem, dve_gdn.mark(("rhs", 2 + g)))
                for g in range(2):
                    by_head(sq[:, g, :].rearrange("p (h n) -> p h n", h=4), ("qs", g), e_cum[:, 4 * g:4 * g + 4], ("qs", g))
                for g in range(2):
                    by_head(v_new[:, 2 + g, :, :], ("solved", 2 + g), d_k[:, 1, 4 * g:4 * g + 4], ("v_new", 2 + g))
                for g in range(4):
                    c, hh = g // 2, g % 2
                    s4 = slice(4 * hh, 4 * hh + 4)
                    if g >= 2:
                        dve.wait_ge(*act_gdn.at(layer, ("o", g)))
                        V.tensor_tensor(flat(o_tok[:, g, :, :]), flat(o_tok[:, g, :, :]), sq[:, g % 2, :], ALU.add)\
                            .then_inc(dve_gdn.sem, dve_gdn.mark(("o", g)))
                    dve.wait_ge(*act_gdn.at(layer, ("o_sq", g)))
                    link(V.tensor_reduce(oss[:, c, s4], th[:, g % 2, :].rearrange("p (h n) -> p h n", h=4), AX_X, ALU.add), dve_gdn, ("oss", g))
                    V.scalar_tensor_tensor(out=oscale[:, c, s4], in0=oss[:, c, s4], scalar=1.0 / DH, in1=o_eps[:, c, s4],
                                           op0=ALU.mult, op1=ALU.add).then_inc(dve_gdn.sem, dve_gdn.mark(("o_mean", g)))
                for g in range(4):
                    c, hh = g // 2, g % 2
                    dve.wait_ge(*pool_gdn.at(layer, ("o_scale", g)))
                    V.tensor_tensor(o_tok[:, g, :, :], o_tok[:, g, :, :], cols(oscale[:, c, 4 * hh:4 * hh + 4], P), ALU.mult)\
                        .then_inc(dve_gdn.sem, dve_gdn.mark(("o_norm", g)))
                for j in range(G_HEADS // 2):
                    dve.wait_ge(*pe_gdn.at(layer, ("yb", j)))
                    dve.wait_ge(*act_gate.at(layer, ("gb", j)))
                    link(V.scalar_tensor_tensor(out=th[:, j % 2, :], in0=flat(gates[:, 8 + 2 * j:10 + 2 * j, :]), scalar=1.0,
                                                in1=bank(("yb", j)), op0=ALU.add, op1=ALU.mult), dve_gdn, ("yb", j))
                    y2 = flat(y[:, 2 * j:2 * j + 2, :])
                    V.scalar_tensor_tensor(out=y2, in0=th[:, j % 2, :], scalar=half_gdn, in1=y2, op0=ALU.mult, op1=ALU.add)\
                        .then_inc(dve_gdn.sem, dve_gdn.mark(("y", j)))
                postnorm("mix", 0)
                prenorm("x", R_X)
                for c in range(TILES):
                    for j in range(2):
                        dve.wait_ge(*pe_x.at(layer, ("xs", c, j)))
                        row_max(bank(("xs", c, j)).rearrange("p (h s) -> p h s", h=2), c, 2 * j, 2, X_DH ** -0.5, ("xmax", c, j))
                for c in range(TILES):
                    for j in range(2):
                        dve.wait_ge(*act_att.at(layer, ("xs", c, j)))
                        normalise(px[:, c, 2 * j:2 * j + 2, :], c, 2 * j, 2, ("px", c, j))
                postnorm("x", 1)
                prenorm("ffn", R_FFN)
                for i in range(FF // 256):
                    dve.wait_ge(*act_ff.at(layer, ("tanh", i)))
                    link(V.scalar_tensor_tensor(out=sq[:, i % 2, :], in0=th[:, i % 2, :], scalar=1.0, in1=bank(("gate", i)),
                                                op0=ALU.add, op1=ALU.mult), dve_ff, ("silu", i))
                    dve.wait_ge(*slots.at(layer, ("up", i)))
                    V.scalar_tensor_tensor(out=flat(ff[:, 2 * i:2 * i + 2, :]), in0=sq[:, i % 2, :], scalar=0.5, in1=bank(("up", i)),
                                           op0=ALU.mult, op1=ALU.mult).then_inc(dve_ff.sem, dve_ff.mark(("ff", i)))
                postnorm("ffn", 2, final=True)


CONV_SLOTS = [(part, i) for part in ("bk", "bq", "bv") for i in range(4)]
LAST = {"out": 3, "xo": 3, "down": FF_BLOCKS // 2 - 1}


def mem_block(t):
    return t[:, :].rearrange("p (c d) -> p c d", c=TILES)


def flat(ap):
    return ap.rearrange("p a b -> p (a b)")


def constants():
    i = np.arange(P)
    c = np.zeros((P, N_CONST), np.float32)
    c[:, C_IDENT:C_IDENT + P] = np.eye(P)
    c[:, C_AFTER:C_AFTER + P] = i[:, None] > i[None, :]
    c[:, C_UPTO:C_UPTO + P] = i[:, None] <= i[None, :]
    c[:, C_MASK1:C_MASK1 + P] = (i[None, :] == i[:, None] + 1) & (i[:, None] % 2 == 0)
    c[:, C_IDXBIAS:C_IDXBIAS + P] = np.where(i[None, :] > i[:, None], NEG, 0.0)
    for n, s in enumerate(LEVELS):
        k = np.concatenate([np.arange(2 * s * b, 2 * s * b + s) for b in range(P // (2 * s))])
        c[:, C_LEVEL + 64 * n:C_LEVEL + 64 * (n + 1)] = i[:, None] // s == k[None, :] // s + 1
    for col, sgn, d in ((C_INV_A, C_SGN_A, DH), (C_INV_I, C_SGN_I, IDX_DIM)):
        inv = np.float32(THETA) ** (-np.arange(d // 2, dtype=np.float32) * np.float32(2) / np.float32(d))
        c[:, col] = inv[i % (d // 2)]
        c[:, sgn] = np.where(i % d < d // 2, 1.0, -1.0)
    c[:, C_ONE] = 1.0
    c[:, C_EPS] = EPS
    c[:, C_NEGHALF:] = -0.5
    b = np.zeros((P, 5 * P), np.float32)
    b[:, 0:P] = np.eye(P)
    b[:, P:] = np.tile(np.where(i[None, :] < i[:, None], NEG, 0.0), (1, 4))
    return c, b.astype(mybir.dt.np(BF16))


def lay_out(inputs):
    w = {k: np.asarray(v) for k, v in inputs.items()}
    stream = np.zeros((DEPTH, SLOTS, P, SLOT), np.float32)
    wide = lambda m: m.reshape(KT, P, -1).transpose(1, 0, 2)
    for layer in range(DEPTH):
        w_in = w["w_in"][layer]
        part = lambda name: w_in[:, COL[name]:COL[name] + SIZES[name]]
        small = wide(np.concatenate([part("ik"), part("ik"), part("iw"), part("ba"), part("bb")], 1))
        mats = {**{k: part(k) for k in ("iq", "k", "v", "q", "bq", "bk", "bv", "ga", "gb")},
                "xk": w["w_xkv"][layer][:, 0:D], "xq": w["w_xq"][layer],
                "gate": w["w_gu"][layer][:, 0:FF], "up": w["w_gu"][layer][:, FF:]}
        tall = {"out": w["w_out"][layer], "xo": w["w_xo"][layer], "xv": w["w_xkv"][layer][:, D:]}
        for n, (name, i) in enumerate(STREAM):
            if name == "small":
                stream[layer, n].reshape(P, KT, 256)[:, :, 0:small.shape[2]] = small
            elif name == "down":
                stream[layer, n] = w["w_down"][layer][256 * i:256 * (i + 1)].reshape(2, P, D).transpose(1, 0, 2).reshape(P, SLOT)
            elif name in tall:
                m = tall[name][512 * (i % 2):512 * (i % 2 + 1), 512 * (i // 2):512 * (i // 2 + 1)]
                stream[layer, n] = m.reshape(4, P, 512).transpose(1, 0, 2).reshape(P, SLOT)
            else:
                stream[layer, n] = wide(mats[name][:, 256 * i:256 * (i + 1)]).reshape(P, SLOT)
    params = np.zeros((DEPTH + 1, P, N_PARAM), np.float32)
    for layer in range(DEPTH):
        p = params[layer]
        taps = w["conv_w"][layer].reshape(CONV_K, 3, D)[:, [1, 0, 2]]
        p[:, R_CONV:R_CONV + 96] = taps.reshape(CONV_K * 24, P).T
        for col, name in ((R_MIX, "norm_mix_pre"), (R_X, "norm_x_pre"), (R_MEM, "norm_mem"), (R_FFN, "norm_ffn_pre")):
            p[:, col:col + KT] = w[name][layer].reshape(KT, P).T
        p[:, R_GDN] = w["gdn_norm"][layer]
        p[:, R_DT:R_DT + 8] = w["dt_bias"][layer][None, :]
        p[:, R_ALOG:R_ALOG + 8] = w["a_log"][layer][None, :]
    post = np.zeros((3 * DEPTH + 1, D), np.float32)
    for layer in range(DEPTH):
        for row, name in enumerate(("norm_mix_post", "norm_x_post", "norm_ffn_post")):
            post[3 * layer + row] = w[name][layer]
    return stream.reshape(DEPTH * SLOTS, P, SLOT), params, post


def kernel(**inputs):
    import concourse.bacc as bacc
    from concourse.bass_utils import run_bass_kernel_spmd

    weights, params, post = lay_out(inputs)
    consts, consts_b = constants()
    arrays = {"x": np.asarray(inputs["x"])[0], "mem": np.asarray(inputs["mem"])[0], "positions": np.asarray(inputs["positions"]),
              "weights": weights, "params": params, "post_gains": post, "consts": consts, "consts_b": consts_b}
    plan = Plan()
    for _ in range(2):
        nc = bacc.Bacc("TRN2", target_bir_lowering=False, num_devices=1)
        args = [nc.dram_tensor(n, a.shape, mybir.dt.from_np(a.dtype), kind="ExternalInput").ap() for n, a in arrays.items()]
        out = nc.dram_tensor("out", (S, D), F32, kind="ExternalOutput").ap()
        nc.disable_value_cache = True
        program(nc, plan, *args, out)
    r = run_bass_kernel_spmd(nc, [arrays], core_ids=[0])
    return r.results[0]["out"][None]
```

```python
from contextlib import ExitStack

import numpy as np

import concourse.bass as bass
from concourse import mybir

ALU = mybir.AluOpType
ACT = mybir.ActivationFunctionType
AX_X = mybir.AxisListType.X
F32 = mybir.dt.float32
F32R = mybir.dt.float32r
BF16 = mybir.dt.bfloat16
I32 = mybir.dt.int32

P = 128
D = 1024
KT = D // P
S = 256
TILES = S // P
DEPTH = 2
EPS = 1e-6
THETA = 10000.0
HEADS, KV_HEADS, DH = 8, 2, 128
IDX_HEADS, IDX_DIM = 4, 64
TOPK = min(256, S // 4)
CONV_K = 4
G_HEADS = 8
X_HEADS = 4
X_DH = D // X_HEADS
FF = -(-8 * D // (3 * 256)) * 256
FF_BLOCKS = FF // P
NEG = -1.0e30
TAKEN = -3.0e38

SIZES = dict(q=HEADS * DH, k=KV_HEADS * DH, v=KV_HEADS * DH, iq=IDX_HEADS * IDX_DIM, ik=IDX_DIM, iw=IDX_HEADS,
             bq=D, bk=D, bv=D, ba=G_HEADS, bb=G_HEADS, ga=D, gb=D)
COL = dict(zip(SIZES, np.cumsum([0] + list(SIZES.values())[:-1]).tolist()))

HALF = KT * P
FF_SLOTS = FF // 256
STREAM = (
    [("xk", i) for i in range(3)] + [("iq", 0), ("small", 0), ("k", 0), ("v", 0)]
    + [("q", i) for i in range(4)]
    + [("bk", i) for i in range(4)] + [("bq", i) for i in range(4)] + [("bv", i) for i in range(4)]
    + [("ga", i) for i in range(4)] + [("gb", i) for i in range(4)]
    + [("xk", 3), ("xv", 0)] + [("out", i) for i in range(4)] + [("xv", i) for i in range(1, 4)]
    + [("xq", i) for i in range(4)] + [("xo", i) for i in range(4)]
    + [step for i in range(FF_SLOTS) for step in [("gate", i), ("up", i)] + ([("down", i - 1)] if i else [])]
    + [("down", FF_SLOTS - 1)]
)
HALVES = 2 * len(STREAM)
RING = 3
VECTOR_SPLITS = 2
assert HALVES % RING == 0
HALF_AT = {key: 2 * n for n, key in enumerate(STREAM)}

C_IDENT, C_AFTER, C_UPTO, C_MASK1, C_IDXBIAS = 0, 128, 256, 384, 512
C_LEVEL = 640
LEVELS = (2, 4, 8, 16, 32, 64)
C_INV_A = C_LEVEL + 64 * len(LEVELS)
C_INV_I, C_SGN_A, C_SGN_I, C_ONE = C_INV_A + 1, C_INV_A + 2, C_INV_A + 3, C_INV_A + 4
C_EPS = C_ONE + 1
C_NEGHALF = C_EPS + 1
N_CONST = C_NEGHALF + 16
R_CONV, R_MEM, R_GDN, R_DT, R_ALOG = 0, 96, 104, 105, 113
N_PARAM = 121

PI = 3.141592653589793
TWO_PI_1 = 6.28125
TWO_PI_2 = 2029.0 / 2 ** 20
TWO_PI_3 = 2 * PI - TWO_PI_1 - TWO_PI_2
PI_BELOW = 3.1415925
ROUND = 12582912.0


SBUF_START, SBUF_END = 16512, 229312


class Plan:

    def __init__(self):
        self.marks, self.totals, self.banks = {}, {}, {}
        self.after = {}


class Steps:

    def __init__(self, plan, sem, name, before=0):
        self.plan, self.sem, self.name, self.before, self.count = plan, sem, name, before, 0

    def mark(self, what):
        self.count += 1
        self.plan.marks[self.name, what] = self.count
        self.plan.totals[self.name] = max(self.count, self.plan.totals.get(self.name, 0))
        return 1

    def at(self, layer, what):
        return self.sem, self.before + layer * self.plan.totals.get(self.name, 1) + self.plan.marks.get((self.name, what), 1)


def program(nc, plan, x_in, mem_in, pos_in, weights, params, pre_gains, post_gains, consts, consts_b, out):
    with ExitStack() as ctx:
        top = [SBUF_START]

        def sb(name, cols, dt=F32, at=None, skip=0):
            start = top[0] if at is None else places[at.name] + 4 * skip
            t = nc.alloc_sbuf_tensor_at(f"sb_{name}", [P, cols], dt, offset=start, align_bytes=32)
            places[t.name] = start
            size = -(-cols * (2 if dt == BF16 else 4) // 32) * 32
            top[0] = max(top[0], start + size)
            assert top[0] <= SBUF_END, top[0]
            return t

        places = {}

        def steps(name, before=0):
            return Steps(plan, ctx.enter_context(nc.semaphore(name)), name, before)

        def sem(name):
            return ctx.enter_context(nc.semaphore(name))

        raw_t = sb("raw", RING * HALF)
        high_t = sb("high", RING * HALF, F32R)
        low_t = sb("low", RING * HALF, F32R)
        x_t = sb("x", TILES * D)
        mem_feat_t = sb("mem_feat", D * TILES)
        kx_t = sb("kx", D * TILES)
        vx_t = sb("vx", D * TILES)
        rope_t = sb("rope_tables", 4 * S)
        const_t = sb("const", N_CONST)
        constb_t = sb("const_b", 5 * P, BF16)
        param_t = sb("param", N_PARAM)
        h_high_t = sb("h_high", D * TILES, F32R)
        h_low_t = sb("h_low", D * TILES, F32R)
        h_t = sb("h_place", D * TILES, F32, h_high_t)
        y_t = sb("y", D * TILES)
        gates_t = sb("gates", 2 * D * TILES)
        conv_t = sb("conv", 3 * D * TILES)
        th_t = sb("th", 1024)
        sq_t = sb("sq", 1024)
        decay_t = sb("decay", 2048)
        attn_t = sb("attn", 2048)
        m_t = sb("m", 2048)
        ra_t = sb("region_a", 2048)
        rb_t = sb("region_b", 2048)
        rc_t = sb("region_c", 1024)
        kd_t = sb("k_rope", KV_HEADS * S)
        v_t = sb("v", KV_HEADS * S)
        selb_t = sb("sel_bias", TILES * S, BF16, conv_t, 2 * D * TILES)
        pre_gain_t = sb("pre_gain", D, F32, gates_t, 3 * D)
        mem_high_t = sb("mem_high", D * TILES, F32R, conv_t, 2 * D * TILES)
        mem_low_t = sb("mem_low", D * TILES, F32R)
        tiny_t = sb("tiny", 480)
        gain_t = sb("post_gain", D, F32, rc_t)
        y_high_t, y_low_t = sb("y_high", D * TILES, F32R, rb_t), sb("y_low", D * TILES, F32R, decay_t)
        ox_high_t, ox_low_t = sb("ox_high", D * TILES, F32R, attn_t), sb("ox_low", D * TILES, F32R, m_t)
        ff_t = sb("ff", 2 * 3 * 512, F32R, gates_t)
        psum = ctx.enter_context(nc.psum_tensor("psum", [P, 8, 512], F32))

        raw, high, low = (t[:, :].rearrange("p (r n) -> p r n", r=RING) for t in (raw_t, high_t, low_t))
        x = x_t[:, :].rearrange("p (c d) -> p c d", c=TILES)
        feat = lambda t: t[:, 0:D * TILES].rearrange("p (k t) -> p k t", t=S)
        mem_feat, kx, y = feat(mem_feat_t), feat(kx_t), feat(y_t)
        h = feat(h_high_t), feat(h_low_t)
        mem_gain = feat(mem_high_t), feat(mem_low_t)
        y_parts = feat(y_high_t), feat(y_low_t)
        ox = feat(ox_high_t), feat(ox_low_t)
        ff = tuple(ff_t[:, n:n + 3 * 512].rearrange("p (r k t) -> p r k t", r=3, k=2) for n in (0, 3 * 512))
        vx = vx_t[:, :].rearrange("p (c d) -> p c d", c=TILES)
        rope = rope_t[:, :].rearrange("p (w t) -> p w t", w=4)
        ident = const_t[:, C_IDENT:C_IDENT + P]
        after = const_t[:, C_AFTER:C_AFTER + P]
        upto = const_t[:, C_UPTO:C_UPTO + P]
        mask1 = const_t[:, C_MASK1:C_MASK1 + P]
        idx_bias = const_t[:, C_IDXBIAS:C_IDXBIAS + P]
        one = const_t[:, C_ONE:C_ONE + 1]
        eps_col = const_t[:, C_EPS:C_EPS + 1]
        neghalf = const_t[:, C_NEGHALF:C_NEGHALF + 16]
        ident_b = constb_t[:, 0:P]
        decay_bias = constb_t[:, P:5 * P]
        gates = gates_t[:, :].rearrange("p (k t) -> p k t", t=S)
        conv = conv_t[:, :].rearrange("p (k t) -> p k t", t=S)
        th = th_t[:, :].rearrange("p (b n) -> p b n", b=2)
        sq = sq_t[:, :].rearrange("p (b n) -> p b n", b=2)
        grp = lambda t: t[:, 0:2048].rearrange("p (g h n) -> p g h n", g=4, h=4)
        decay, attn, m_up = grp(decay_t), grp(attn_t), grp(m_t)
        xn = ra_t[:, :].rearrange("p (c d) -> p c d", c=TILES)
        idx_relu = ra_t[:, 0:1024].rearrange("p (h s) -> p h s", h=IDX_HEADS)
        idx_val = ra_t[:, 1024:1536].rearrange("p (c s) -> p c s", c=TILES)
        iq = rb_t[:, 0:512].rearrange("p (b t) -> p b t", b=2)
        ik = rb_t[:, 512:768]
        rope_tmp = rc_t[:, 0:1024].rearrange("p (b n) -> p b n", b=2)
        p1 = ra_t[:, :].rearrange("p (h s) -> p h s", h=HEADS)
        t_up = grp(ra_t)
        q = gates_t[:, 0:2048].rearrange("p (h t) -> p h t", h=HEADS)
        pt0 = rb_t[:, :].rearrange("p (h t) -> p h t", h=HEADS)
        t_low = grp(rb_t)
        p0 = y_t[:, 0:1024].rearrange("p (h s) -> p h s", h=HEADS)
        pt1 = rc_t[:, :].rearrange("p (h t) -> p h t", h=HEADS)
        prod = rc_t[:, :].rearrange("p (g h n) -> p g h n", g=4, h=4)
        g_after = vx_t[:, :].rearrange("p (c h n) -> p c h n", c=TILES, h=G_HEADS)
        rhs = grp(vx_t)
        v_new = grp(decay_t)
        k_dec = h_t[:, 0:1024].rearrange("p (h n) -> p h n", h=G_HEADS)
        state = h_t[:, 1024:2048].rearrange("p (h n) -> p h n", h=G_HEADS)
        o_tok = grp(m_t)
        kT = kd_t[:, :].rearrange("p (g t) -> p g t", g=KV_HEADS)
        v_tok = v_t[:, :].rearrange("p (c d) -> p c d", c=TILES)
        sel_bias = selb_t[:, :].rearrange("p (c s) -> p c s", c=TILES)
        qx = gates_t[:, 0:2048].rearrange("p (k t) -> p k t", t=S)
        px = gates_t[:, 2048:4096].rearrange("p (c h s) -> p c h s", c=TILES, h=X_HEADS)
        pxt = decay_t[:, :].rearrange("p (b h t) -> p b h t", b=TILES, h=X_HEADS)

        tiny_at = [0]

        def tiny(n):
            tiny_at[0] += n
            assert tiny_at[0] <= 480
            return tiny_t[:, tiny_at[0] - n:tiny_at[0]]

        ss, rs = tiny(2), tiny(2)
        ss2, rs2 = tiny(2), tiny(2)
        ss2a, more = tiny(2), tiny(2)
        small = tiny(2 * 20).rearrange("p (c n) -> p c n", c=TILES)
        two = lambda: tiny(16).rearrange("p (c h) -> p c h", c=TILES)
        ga_x, ga_abs, ga_e, ga_w, ga_ln, ga_t, ga_r, g_tok, beta = (two() for _ in range(9))
        a_exp = tiny(8)
        top8 = tiny(8)
        e_last, e_cum = tiny(8), tiny(8)
        ss_kq = tiny(32).rearrange("p (c b) -> p c b", c=TILES)
        rk, v_scale, d_k, m_scale, o_eps, k_scale0 = two(), two(), two(), two(), two(), tiny(8)
        half_gdn = tiny(1)
        mx, nmx, psumr, pinv = (tiny(16).rearrange("p (c h) -> p c h", c=TILES) for _ in range(4))
        oss, oscale = two(), two()

        raw_loaded = [sem(f"raw_loaded_{k}") for k in range(RING)]
        high_ready = sem("high_ready")
        low_ready = [sem(f"low_ready_{k}") for k in range(RING)]
        consts_loaded, x_loaded, mem_loaded, pos_loaded = (sem(f"{n}_loaded") for n in ("consts", "x", "mem", "pos"))
        tables_act = sem("tables_act")
        mem_act, mem_pool, mem_dve, mem_pe = (sem(f"mem_{n}") for n in ("act", "pool", "dve", "pe"))
        out_stored = sem("out_stored")
        param_loaded = sem("param_loaded")
        gain_loaded = sem("gain_loaded")
        slots = steps("slots", RING)
        mem_high_ready, mem_low_ready = sem("mem_high_ready"), sem("mem_low_ready")
        dve_part, act_part = steps("dve_part"), steps("act_part")
        pe_t = steps("pe_transposed")
        pe_idx = steps("pe_idx")
        pe_att = steps("pe_att")
        pe_gdn = steps("pe_gdn")
        pe_x = steps("pe_xattn")
        pe_out = steps("pe_out_tile0")
        act_norm = steps("act_norm")
        act_copy = steps("act_copy")
        act_gate = steps("act_gate")
        act_conv = steps("act_conv")
        act_att = steps("act_att")
        act_gdn = steps("act_gdn")
        act_ff = steps("act_ff")
        dve_norm = steps("dve_norm")
        dve_rope = steps("dve_rope")
        dve_gate = steps("dve_gate")
        dve_idx = steps("dve_idx")
        dve_conv = steps("dve_conv")
        dve_att = steps("dve_att")
        dve_gdn = steps("dve_gdn")
        dve_ff = steps("dve_ff")
        pool_norm = steps("pool_norm")
        x_ready = sem("x_ready")
        table = steps("table")
        pool_gdn = steps("pool_gdn")
        pool_part = steps("pool_part")
        pre_loaded = sem("pre_loaded")

        def bank(what):
            return psum[:, plan.banks.get(what, 0), :]

        def angle(w):
            return y_t[:, (2 + w) * S:(3 + w) * S]

        def tap(k, block):
            col = R_CONV + 24 * k + block
            return param_t[:, col:col + 1]

        def junk(c):
            return (sq_t, th_t)[c][:, :]

        def y_tile(c):
            return psum[:, 4 + 2 * c:6 + 2 * c, :].rearrange("p b n -> p (b n)")

        def cols(ap, n):
            m = ap.shape[-1]
            return ap.unsqueeze(2).broadcast_to([P, m, n])

        def heads(ap, m):
            return ap.unsqueeze(1).broadcast_to([P, m, ap.shape[-1]])

        def even(t, s):
            return t.rearrange("p h (b w c) -> p (h b) w c", w=2, c=s)[:, :, 0, :]

        def highs(act, layer, done, upto):
            for n in range(done[0], min(upto, HALVES + RING)):
                k = n % RING
                act.wait_ge(raw_loaded[k], 16 * (layer * (HALVES // RING) + n // RING + 1))
                act.wait_ge(slots.sem, layer * HALVES + n + 1)
                nc.scalar.activation(high[:, k, :], raw[:, k, :], ACT.Copy).then_inc(high_ready, 1)
                done[0] = n + 1

        def lows(eng, layer, done, upto, places):
            for n in range(done[0], min(upto, HALVES + RING)):
                k = n % RING
                if k in places:
                    eng.wait_ge(high_ready, layer * HALVES + n + 1)
                    eng.tensor_tensor(low[:, k, :], raw[:, k, :], high[:, k, :].bitcast(F32), ALU.subtract).then_inc(low_ready[k], 1)
                done[0] = n + 1

        def ahead(what, extra):
            return plan.after.get(what, 0) + extra

        def y_low(eng, layer, done, j):
            eng.wait_ge(*act_part.at(layer, ("y", j)))
            eng.tensor_tensor(flat(y_parts[1][:, 2 * j:2 * j + 2, :]), flat(y[:, 2 * j:2 * j + 2, :]),
                              flat(y_parts[0][:, 2 * j:2 * j + 2, :]).bitcast(F32), ALU.subtract).then_inc(done.sem, done.mark(("y_low", j)))

        block = ctx.enter_context(nc.Block())

        @block.sync
        def _(sp):
            sp.dma_start(mem_block(kx_t), mem_in.rearrange("(c p) d -> p c d", p=P)).then_inc(mem_loaded, 16)
            sp.dma_start(const_t[:, :], consts).then_inc(consts_loaded, 16)
            sp.dma_start(constb_t[:, :], consts_b).then_inc(consts_loaded, 16)
            sp.dma_start(x, x_in.rearrange("(c p) d -> p c d", p=P)).then_inc(x_loaded, 16)
            sp.dma_start(y_t[:, 0:S].bitcast(I32), pos_in.broadcast_to([P, S])).then_inc(pos_loaded, 16)
            for k in range(RING):
                sp.dma_start(raw[:, k, :], weights[k]).then_inc(raw_loaded[k], 16)
            with sp.Fori(1, DEPTH * HALVES // RING + 1) as r:
                for k in range(RING):
                    sp.wait_ge(low_ready[k], r)
                    sp.dma_start(raw[:, k, :], weights[bass.ds(r * RING + k, 1), :, :].rearrange("a p n -> p (a n)"))\
                        .then_inc(raw_loaded[k], 16)
            sp.wait_ge(x_ready, TILES * (DEPTH + 1))
            sp.dma_start(out.rearrange("(c p) d -> p c d", p=P), x).then_inc(out_stored, 16)
            sp.wait_ge(out_stored, 16)

        @block.tensor
        def _(pe):
            pe.wait_ge(consts_loaded, 32)
            pe.transpose(psum[:, 4, 0:P], ident, ident).then_inc(slots.sem, RING)
            for j in range(4):
                c, half = j // 2, j % 2
                pe.wait_ge(mem_dve, c + 1)
                for k in range(4):
                    tr = pe.transpose(psum[:, j, k * P:(k + 1) * P], mem_block(kx_t)[:, c, (4 * half + k) * P:(4 * half + k + 1) * P], ident)
                tr.then_inc(mem_pe, 1)

            with pe.Fori(0, DEPTH) as layer:
                last = {}
                turn = [0]
                used = [0]

                def mark(done, what):
                    plan.after[what] = used[0]
                    return done.mark(what)

                def claim(what, reader, banks=range(7)):
                    b = min(banks, key=lambda b: ((b - turn[0]) % 8))
                    turn[0] = (b + 1) % 8
                    if b in last:
                        pe.wait_ge(*last[b][0].at(layer, last[b][1]))
                    last[b] = reader
                    plan.banks[what] = b
                    return psum[:, b, :]

                def weights_here(n):
                    assert n == used[0]
                    used[0] = n + 1
                    pe.wait_ge(low_ready[n % RING], layer * (HALVES // RING) + n // RING + 1)
                    return high[:, n % RING, :], low[:, n % RING, :]

                def product(out, a, b, start, stop, **kw):
                    pe.matmul(out, a[0], b[0], start=start, stop=False, **kw)
                    pe.matmul(out, a[0], b[1], start=False, stop=False, **kw)
                    return pe.matmul(out, a[1], b[0], start=False, stop=stop, **kw)

                def pick(parts, f):
                    return f(parts[0]), f(parts[1])

                def wide_half(o, n, act):
                    w = weights_here(n)
                    for k in range(KT):
                        mm = product(o, pick(w, lambda t: t[:, k * P:(k + 1) * P]), pick(act, lambda t: t[:, k, :]), k == 0, k == KT - 1)
                    return mm

                def wide(key, act, reader, banks=range(7)):
                    o = claim(key, reader, banks)
                    for b in range(2):
                        mm = wide_half(o[:, b * S:(b + 1) * S], HALF_AT[key] + b, act)
                        mm.then_inc(slots.sem, mark(slots, key if b else (key, "first")))

                def tall(part, i, act, outs):
                    for b in range(2):
                        w = weights_here(HALF_AT[part, i] + b)
                        for c in range(TILES):
                            for k2 in range(2):
                                k = 4 * (i % 2) + 2 * b + k2
                                mm = product(outs[c], pick(act, lambda t: t[:, k, c * P:(c + 1) * P]),
                                             pick(w, lambda t: t[:, k2 * 512:(k2 + 1) * 512]), k == 0, k == KT - 1)
                            if c == 0 and i == 3 and b == 1:
                                mm.then_inc(pe_out.sem, mark(pe_out, part))
                        mm.then_inc(slots.sem, mark(slots, (part, i) if b else ((part, i), "first")))

                def norm_transposes(which):
                    for c in range(TILES):
                        pe.wait_ge(*dve_norm.at(layer, ("xn", which, c)))
                        for half in range(2):
                            what = ("h", which, c, half)
                            o = claim(what, (dve_part, ("h_low", which, c, half)), range(4, 8))
                            for k in range(4):
                                b = 4 * half + k
                                tr = pe.transpose(o[:, k * P:(k + 1) * P], xn[:, c, b * P:(b + 1) * P], ident)
                            tr.then_inc(pe_t.sem, mark(pe_t, what))

                pe.wait_ge(mem_low_ready, layer + 1)
                for i in range(2):
                    wide(("xk", i), mem_gain, (act_copy, ("xk", i)), range(4))
                norm_transposes("mix")
                wide(("xk", 2), mem_gain, (act_copy, ("xk", 2)), range(4))
                pe.wait_ge(*dve_part.at(layer, ("h_low", "mix", 1, 1)))
                wide(("iq", 0), h, (dve_rope, "iq"))
                o = claim(("small", 0), (act_copy, "small"))
                n = HALF_AT["small", 0]
                wide_half(o[:, 0:S], n, h).then_inc(slots.sem, mark(slots, "ik"))
                w = weights_here(n + 1)
                for c in range(TILES):
                    for k in range(KT):
                        mm = product(o[:, S + 20 * c:S + 20 * c + 20], pick(h, lambda t: t[:, k, c * P:(c + 1) * P]),
                                     pick(w, lambda t: t[:, k * P:k * P + 20]), k == 0, k == KT - 1)
                mm.then_inc(slots.sem, mark(slots, ("small", 0)))
                wide(("k", 0), h, (dve_rope, "k"))
                o = claim(("v", 0), (act_copy, "v"))
                for b in range(2):
                    w = weights_here(HALF_AT["v", 0] + b)
                    for c in range(TILES):
                        for k4 in range(4):
                            k = 4 * b + k4
                            mm = product(o[:, c * 256:(c + 1) * 256], pick(h, lambda t: t[:, k, c * P:(c + 1) * P]),
                                         pick(w, lambda t: t[:, k4 * 256:(k4 + 1) * 256]), k == 0 and c == 0, k == KT - 1 and c == 1,
                                         skip_group_check=True)
                    mm.then_inc(slots.sem, mark(slots, ("v", 0) if b else ("v", "first")))
                wide(("q", 0), h, (dve_rope, ("q", 0)))
                pe.wait_ge(*dve_rope.at(layer, "iq"))
                pe.wait_ge(*dve_rope.at(layer, "ik"))
                for c in range(TILES):
                    keys = (c + 1) * P
                    for odd in range(2):
                        what = ("logits", c, odd)
                        o = claim(what, (act_att, what))
                        lo = 64 * odd
                        for b in range(2):
                            mm = pe.matmul(o[:, b * keys:(b + 1) * keys], iq[lo:lo + 64, b, c * P:(c + 1) * P],
                                           ik[lo:lo + 64, 0:keys], start=True, stop=True)
                        mm.then_inc(pe_idx.sem, mark(pe_idx, what))
                for i in range(1, 4):
                    wide(("q", i), h, (dve_rope, ("q", i)))
                misc = psum[:, 7, :]
                last[7] = (dve_gdn, "ss")
                for c in range(TILES):
                    pe.wait_ge(*dve_gate.at(layer, ("g_after", c)))
                    for hh in range(2):
                        what = ("decay", c, hh)
                        o = claim(what, (act_gdn, what))
                        pe.matmul(o, ident_b, decay_bias, start=True, stop=False, skip_group_check=True)
                        for hd in range(4):
                            mm = pe.matmul(o[:, hd * P:(hd + 1) * P], g_after[:, c, 4 * hh + hd, :], upto,
                                           start=False, stop=(hd == 3), skip_group_check=True)
                        mm.then_inc(pe_gdn.sem, mark(pe_gdn, what))
                pe.matmul(misc[:, 32:40], after, g_tok[:, 0, :], start=True, stop=True)
                pe.matmul(misc[:, 40:48], upto, g_tok[:, 1, :], start=True, stop=True)\
                    .then_inc(pe_gdn.sem, mark(pe_gdn, "g_sums"))

                def squares(j):
                    pe.wait_ge(*act_conv.at(layer, ("sq", j)))
                    for b in range(2):
                        for c in range(TILES):
                            mm = pe.matmul(misc[:, 16 * c + 2 * j + b:16 * c + 2 * j + b + 1],
                                           sq[:, j % 2, b * S + c * P:b * S + (c + 1) * P], one, start=True, stop=True)
                    mm.then_inc(pe_gdn.sem, mark(pe_gdn, ("squares", j)))

                for i in range(4):
                    wide(("bk", i), h, (dve_conv, ("tap", 0, i)))
                    if i == 3:
                        pe.wait_ge(*act_gdn.at(layer, "e_cum"))
                        squares(0)
                for c in range(TILES):
                    pe.wait_ge(*dve_idx.at(layer, ("bias", c)))
                    pe.wait_ge(*dve_rope.at(layer, ("q", 3)))
                    keys, n_h = (c + 1) * P, 4 // (c + 1)
                    for j in range(HEADS // n_h):
                        what = ("scores", c, j)
                        o = claim(what, (act_att, what))
                        for i in range(n_h):
                            hd = n_h * j + i
                            pe.matmul(o[:, i * keys:(i + 1) * keys], q[:, hd, c * P:(c + 1) * P],
                                      kT[:, hd // (HEADS // KV_HEADS), 0:keys], start=True, stop=False, skip_group_check=True)
                            mm = pe.matmul(o[:, i * keys:(i + 1) * keys], ident_b, sel_bias[:, c, 0:keys],
                                           start=False, stop=True, skip_group_check=True)
                        mm.then_inc(pe_att.sem, mark(pe_att, what))
                for i in range(4):
                    wide(("bq", i), h, (dve_conv, ("tap", 0, 4 + i)))
                    squares(1 + i)
                for j in range(HEADS // 2):
                    what = ("pt0", j)
                    o = claim(what, (act_att, what))
                    pe.wait_ge(*dve_att.at(layer, ("p", 0, j // 2)))
                    pe.wait_ge(*dve_att.at(layer, ("p", 1, j)))
                    for i in range(2):
                        pe.transpose(o[:, i * S:i * S + P], p0[:, 2 * j + i, :], ident)
                        tr = pe.transpose(o[:, i * S + P:(i + 1) * S], p1[:, 2 * j + i, 0:P], ident)
                    tr.then_inc(pe_att.sem, mark(pe_att, what))
                for j in range(HEADS // 4):
                    what = ("pt1", j)
                    o = claim(what, (act_att, what))
                    for i in range(4):
                        tr = pe.transpose(o[:, i * P:(i + 1) * P], p1[:, 4 * j + i, P:S], ident)
                    tr.then_inc(pe_att.sem, mark(pe_att, what))
                for i in range(4):
                    wide(("bv", i), h, (dve_conv, ("tap", 0, 8 + i)))
                    if i < 3:
                        squares(5 + i)

                for g in range(4):
                    c, hh = g // 2, g % 2
                    if g == 0:
                        pe.wait_ge(*dve_conv.at(layer, ("silu", 7)))
                    for kind, other in (("kk", 0), ("kq", 8)):
                        what = (kind, g)
                        o = claim(what, (dve_gdn, what))
                        for i in range(4):
                            hd = 4 * hh + i
                            mm = pe.matmul(o[:, i * P:(i + 1) * P], conv[:, hd, c * P:(c + 1) * P],
                                           conv[:, other + hd, c * P:(c + 1) * P], start=True, stop=True)
                        mm.then_inc(pe_gdn.sem, mark(pe_gdn, what))
                    wide(("ga", g), h, (act_gate, ("ga", g)))
                pe.wait_ge(*act_att.at(layer, ("pt1", 1)))
                pe.wait_ge(*act_copy.at(layer, "v"))
                for j in range(HEADS // 2):
                    what = ("att", j)
                    grp_kv = 2 * j // (HEADS // KV_HEADS)
                    o = claim(what, (dve_att, what))
                    pe.matmul(o, v_tok[:, 0, grp_kv * DH:(grp_kv + 1) * DH], pt0[:, 2 * j:2 * j + 2, :],
                              start=True, stop=False, skip_group_check=True)
                    o2 = o.rearrange("p (h t) -> p h t", h=2)
                    mm = pe.matmul(o2[:, :, P:S], v_tok[:, 1, grp_kv * DH:(grp_kv + 1) * DH], pt1[:, 2 * j:2 * j + 2, :],
                                   start=False, stop=True, skip_group_check=True)
                    mm.then_inc(pe_att.sem, mark(pe_att, what))
                for g in range(4):
                    wide(("gb", g), h, (act_gate, ("gb", g)))
                    c, hh = g // 2, g % 2
                    what = ("v_tok", g)
                    o = claim(what, (dve_gdn, what))
                    if g == 0:
                        pe.wait_ge(*dve_conv.at(layer, ("silu", 11)))
                    for i in range(4):
                        tr = pe.transpose(o[:, i * P:(i + 1) * P], conv[:, 16 + 4 * hh + i, c * P:(c + 1) * P], ident)
                    tr.then_inc(pe_gdn.sem, mark(pe_gdn, what))
                for hh in range(2):
                    what = ("k_tok", hh)
                    o = claim(what, (dve_gdn, what))
                    for i in range(4):
                        tr = pe.transpose(o[:, i * P:(i + 1) * P], conv[:, 4 * hh + i, 0:P], ident)
                    tr.then_inc(pe_gdn.sem, mark(pe_gdn, what))
                for g in range(4):
                    what = ("t_low", 1, g)
                    o = claim(what, (act_gdn, what))
                    pe.wait_ge(*dve_gdn.at(layer, ("t_up", g)))
                    for i in range(4):
                        tr = pe.transpose(o[:, i * P:(i + 1) * P], t_up[:, g, i, :], ident)
                    tr.then_inc(pe_gdn.sem, mark(pe_gdn, what))
                for s in LEVELS:
                    for g in range(4):
                        what = ("mt", s, g)
                        o = claim(what, (dve_gdn, what))
                        if s == LEVELS[0]:
                            pe.wait_ge(*act_gdn.at(layer, ("t_low", 1, g)))
                        else:
                            pe.wait_ge(*dve_gdn.at(layer, ("t_low", s // 2, g)))
                        for i in range(4):
                            mm = pe.matmul(o[:, i * 64:(i + 1) * 64], m_up[:, g, i, :], even(t_low[:, g, i:i + 1, :], s),
                                           start=True, stop=True)
                        mm.then_inc(pe_gdn.sem, mark(pe_gdn, what))
                    for g in range(4):
                        what = ("tmt", s, g)
                        o = claim(what, (dve_gdn, ("t_low", s, g)))
                        pe.wait_ge(*dve_gdn.at(layer, ("mt", s, g)))
                        if s != LEVELS[0]:
                            pe.wait_ge(*act_gdn.at(layer, ("t_up", s // 2, g)))
                        for i in range(4):
                            mm = pe.matmul(o[:, i * 64:(i + 1) * 64], t_up[:, g, i, :], prod[:, g, i, :], start=True, stop=True)
                        mm.then_inc(pe_gdn.sem, mark(pe_gdn, what))
                    for g in range(4):
                        what = ("t_up", s, g)
                        o = claim(what, (act_gdn, what))
                        pe.wait_ge(*dve_gdn.at(layer, ("t_low", s, g)))
                        for i in range(4):
                            tr = pe.transpose(o[:, i * P:(i + 1) * P], t_low[:, g, i, :], ident)
                        tr.then_inc(pe_gdn.sem, mark(pe_gdn, what))

                def solve(g):
                    what = ("solved", g)
                    o = claim(what, (dve_gdn, ("v_new", g)))
                    pe.wait_ge(*act_gdn.at(layer, ("t_up", LEVELS[-1], g)))
                    pe.wait_ge(*dve_gdn.at(layer, ("v_tok" if g < 2 else "rhs", g)))
                    for i in range(4):
                        mm = pe.matmul(o[:, i * P:(i + 1) * P], t_up[:, g, i, :], rhs[:, g, i, :], start=True, stop=True)
                    mm.then_inc(pe_gdn.sem, mark(pe_gdn, what))

                def read_out(g):
                    what = ("o", g)
                    o = claim(what, (act_gdn, ("o", g)))
                    for i in range(4):
                        mm = pe.matmul(o[:, i * P:(i + 1) * P], attn[:, g, i, :], v_new[:, g, i, :], start=True, stop=True)
                    mm.then_inc(pe_gdn.sem, mark(pe_gdn, what))

                for g in range(2):
                    solve(g)
                for g in range(2):
                    what = ("state", g)
                    o = claim(what, (act_gdn, what))
                    pe.wait_ge(*dve_gdn.at(layer, ("v_new", g)))
                    pe.wait_ge(*dve_gdn.at(layer, ("k_tok", g)))
                    for i in range(4):
                        mm = pe.matmul(o[:, i * P:(i + 1) * P], k_dec[:, 4 * g + i, :], v_new[:, g, i, :], start=True, stop=True)
                    mm.then_inc(pe_gdn.sem, mark(pe_gdn, what))
                for g in range(2):
                    what = ("ks", g)
                    o = claim(what, (dve_gdn, what))
                    pe.wait_ge(*act_gdn.at(layer, ("state", g)))
                    for i in range(4):
                        hd = 4 * g + i
                        mm = pe.matmul(o[:, i * P:(i + 1) * P], conv[:, hd, P:S], state[:, hd, :], start=True, stop=True)
                    mm.then_inc(pe_gdn.sem, mark(pe_gdn, what))
                for g in range(2):
                    read_out(g)
                for g in range(2):
                    what = ("qs", g)
                    o = claim(what, (dve_gdn, what))
                    for i in range(4):
                        hd = 4 * g + i
                        mm = pe.matmul(o[:, i * P:(i + 1) * P], conv[:, 8 + hd, P:S], state[:, hd, :], start=True, stop=True)
                    mm.then_inc(pe_gdn.sem, mark(pe_gdn, what))
                for g in range(2, 4):
                    solve(g)
                for g in range(2, 4):
                    pe.wait_ge(*dve_gdn.at(layer, ("v_new", g)))
                    read_out(g)
                pe.wait_ge(mem_high_ready, 2 * layer + 2)
                wide(("xk", 3), mem_gain, (act_copy, ("xk", 3)), range(4))
                for j in range(G_HEADS // 2):
                    what = ("yb", j)
                    o = claim(what, (dve_gdn, what), range(4, 8))
                    if j == 0:
                        for g in range(4):
                            pe.wait_ge(*dve_gdn.at(layer, ("o_norm", g)))
                    for i in range(2):
                        hd = 2 * j + i
                        for c in range(TILES):
                            tr = pe.transpose(o[:, i * S + c * P:i * S + (c + 1) * P], o_tok[:, 2 * c + hd // 4, hd % 4, :], ident)
                    tr.then_inc(pe_gdn.sem, mark(pe_gdn, what))
                def values(i):
                    if i % 2 == 0:
                        xv[i // 2] = [claim(("xv", c, i // 2), (act_copy, ("xv", c, i // 2)), (i + c,)) for c in range(TILES)]
                    tall("xv", i, mem_gain, xv[i // 2])

                xv = {}
                values(0)
                pe.wait_ge(*pool_part.at(layer, ("y_low", 1)))
                y_banks = lambda part: [[claim((part, c, half), (dve_norm, ("x", part, c)), (4 + 2 * c + half,))
                                         for c in range(TILES)] for half in range(2)]
                banks = y_banks("out")
                for i in range(4):
                    if i == 1:
                        pe.wait_ge(*pool_part.at(layer, ("y_low", 2)))
                        pe.wait_ge(*dve_part.at(layer, ("y_low", 3)))
                    tall("out", i, y_parts, banks[i // 2])
                values(1)
                values(2)
                norm_transposes("x")
                values(3)
                pe.wait_ge(*dve_part.at(layer, ("h_low", "x", 1, 1)))
                for i in range(4):
                    wide(("xq", i), h, (act_copy, ("xq", i)), range(4, 8))
                for c in range(TILES):
                    for j in range(2):
                        what = ("xs", c, j)
                        o = claim(what, (act_att, what))
                        pe.wait_ge(*act_copy.at(layer, ("xq", 2 * j + 1)))
                        for i in range(2):
                            hd = 2 * j + i
                            for b in range(2):
                                mm = pe.matmul(o[:, i * S:(i + 1) * S], qx[:, 2 * hd + b, c * P:(c + 1) * P], kx[:, 2 * hd + b, :],
                                               start=(b == 0), stop=(b == 1))
                        mm.then_inc(pe_x.sem, mark(pe_x, what))
                xpt = {(b, j): claim(("xpt", b, j), (act_att, ("xpt", b, j))) for j in range(2) for b in range(2)}
                for c in range(TILES):
                    for j in range(2):
                        pe.wait_ge(*dve_att.at(layer, ("px", c, j)))
                        for b in range(2):
                            for i in range(2):
                                tr = pe.transpose(xpt[b, j][:, i * S + c * P:i * S + (c + 1) * P], px[:, c, 2 * j + i, b * P:(b + 1) * P], ident)
                            if c == 1:
                                tr.then_inc(pe_x.sem, mark(pe_x, ("xpt", b, j)))
                for j in range(4):
                    what = ("ox", j)
                    o = claim(what, (dve_part, ("ox_low", j)))
                    pe.wait_ge(*act_att.at(layer, ("xpt", 1, j // 2)))
                    for i in range(2):
                        for b in range(2):
                            mm = pe.matmul(o[:, i * S:(i + 1) * S], vx[:, b, (2 * j + i) * P:(2 * j + i + 1) * P], pxt[:, b, j, :],
                                           start=(b == 0), stop=(b == 1))
                    mm.then_inc(pe_x.sem, mark(pe_x, what))
                banks = y_banks("xo")
                for i in range(4):
                    if i < 2:
                        pe.wait_ge(*dve_part.at(layer, ("ox_low", 2 * i + 1)))
                    tall("xo", i, ox, banks[i // 2])
                norm_transposes("ffn")
                pe.wait_ge(*dve_part.at(layer, ("h_low", "ffn", 1, 1)))
                def down(i):
                    pe.wait_ge(*dve_part.at(layer, ("ff_low", i)))
                    for k in range(2):
                        w = weights_here(HALF_AT["down", i] + k)
                        for c in range(TILES):
                            for half in range(2):
                                mm = product(down_banks[half][c], pick(ff, lambda t: t[:, i % 3, k, c * P:(c + 1) * P]),
                                             pick(w, lambda t: t[:, half * 512:(half + 1) * 512]), i == 0 and k == 0, i == FF_SLOTS - 1 and k == 1)
                            if c == 0 and i == FF_SLOTS - 1 and k == 1:
                                mm.then_inc(pe_out.sem, mark(pe_out, "down"))
                        mm.then_inc(slots.sem, mark(slots, ("down", i) if k else (("down", i), "first")))

                for i in range(FF_SLOTS):
                    wide(("gate", i), h, (dve_ff, ("silu", i)), range(4))
                    wide(("up", i), h, (dve_ff, ("ff", i)), range(4))
                    if i == 0:
                        down_banks = y_banks("down")
                    else:
                        down(i - 1)
                down(FF_SLOTS - 1)

        @block.scalar
        def _(act):
            act.dma_start(param_t[:, :], params[0]).then_inc(param_loaded, 16)
            act.dma_start(pre_gain_t[:, :], pre_gains[0:1, :].broadcast_to([P, D])).then_inc(pre_loaded, 16)
            act.wait_ge(mem_loaded, 16)
            for c in range(TILES):
                nc.scalar.activation(xn[:, c, :], mem_block(kx_t)[:, c, :], ACT.Square, scale=D ** -0.5, accum_out=ss[:, c:c + 1]).then_inc(mem_act, 1)
            highs(act, 0, [0], RING)
            for j in range(4):
                c, half = j // 2, j % 2
                act.wait_ge(mem_pe, j + 1)
                nc.scalar.activation(mem_feat[:, 4 * half:4 * half + 4, c * P:(c + 1) * P],
                                     psum[:, j, :].rearrange("p (k t) -> p k t", k=4), ACT.Copy).then_inc(mem_act, 1)

            def mem_highs():
                for k in range(KT):
                    ins = nc.scalar.activation(mem_gain[0][:, k, :], mem_feat[:, k, :], ACT.Copy, scale=param_t[:, R_MEM + k:R_MEM + k + 1])
                ins.then_inc(mem_high_ready, 1)

            act.wait_ge(param_loaded, 16)
            act.wait_ge(mem_act, 3 * TILES)
            mem_highs()
            for w in range(4):
                act.wait_ge(*table.at(0, ("angle", w)))
                nc.scalar.activation(rope[:, w, :], angle(w), ACT.Sin).then_inc(tables_act, 1)
            act.wait_ge(mem_pool, 2 * TILES)
            act.wait_ge(mem_act, TILES)

            with act.Fori(0, DEPTH) as layer:
                done = [RING]
                high_parts = lambda upto: highs(act, layer, done, upto)

                def square_x(which, c):
                    nc.scalar.activation(xn[:, c, :], x[:, c, :], ACT.Square, scale=D ** -0.5, accum_out=ss[:, c:c + 1])\
                        .then_inc(act_norm.sem, act_norm.mark(("ss", which, c)))

                def load_pre_gain(row):
                    act.dma_start(pre_gain_t[:, :], pre_gains[bass.ds(layer * 3 + row, 1), :].broadcast_to([P, D]))\
                        .then_inc(pre_loaded, 16)

                def load_gain(row):
                    act.dma_start(gain_t[:, :], post_gains[bass.ds(layer * 3 + row, 1), :].broadcast_to([P, D]))\
                        .then_inc(gain_loaded, 16)

                def h_highs(which):
                    for c in range(TILES):
                        for half in range(2):
                            what = ("h", which, c, half)
                            high_parts(ahead(what, 3))
                            act.wait_ge(*pe_t.at(layer, what))
                            nc.scalar.activation(h[0][:, 4 * half:4 * half + 4, c * P:(c + 1) * P],
                                                 bank(what).rearrange("p (k t) -> p k t", k=4), ACT.Copy).then_inc(act_part.sem, act_part.mark(what))

                def values_out(half):
                    for c in range(TILES):
                        copy(vx[:, c, half * 512:(half + 1) * 512], bank(("xv", c, half)), slots, ("xv", 2 * half + 1), act_copy, ("xv", c, half))

                def half_squares(part, product):
                    high_parts(ahead((product, 1), 3))
                    act.wait_ge(*slots.at(layer, (product, 1)))
                    for c in range(TILES):
                        nc.scalar.activation(junk(c)[:, 0:512], y_tile(c)[:, 0:512], ACT.Square, scale=D ** -0.5, accum_out=ss2a[:, c:c + 1])\
                            .then_inc(act_norm.sem, act_norm.mark(("ss2a", part, c)))

                def post_and_pre_norm(part, product, row, which):
                    start = 0 if product == "down" else 512
                    if start:
                        half_squares(part, product)
                    for c in range(TILES):
                        if c == 0:
                            high_parts(ahead(product, 2))
                            act.wait_ge(*pe_out.at(layer, product))
                        else:
                            high_parts(ahead((product, LAST[product]), 3))
                            act.wait_ge(*slots.at(layer, (product, LAST[product])))
                        if start:
                            act.wait_ge(*act_norm.at(layer, ("ss2a", part, c)))
                        nc.scalar.activation(junk(c)[:, start:D], y_tile(c)[:, start:D], ACT.Square, scale=D ** -0.5, accum_out=ss2[:, c:c + 1])\
                            .then_inc(act_norm.sem, act_norm.mark(("ss2", part, c)))
                    if which is not None:
                        for c in range(TILES):
                            act.wait_ge(*dve_norm.at(layer, ("x", part, c)))
                            square_x(which, c)
                            if part == "mix":
                                high_parts(ahead((product, LAST[product]), 4 + c))
                        act.wait_ge(*dve_norm.at(layer, ("scaled", part, 1)))
                        load_gain(row)
                        if part == "mix":
                            values_out(0)
                        h_highs(which)

                def copy(out, src, producer, what, done, name, **kw):
                    high_parts(ahead(what, 3))
                    act.wait_ge(*producer.at(layer, what))
                    nc.scalar.activation(out, src, ACT.Copy, **kw).then_inc(done.sem, done.mark(name))

                for c in range(TILES):
                    act.wait_ge(x_ready, layer * TILES + c + 1)
                    square_x("mix", c)
                def keys_out(i):
                    copy(flat(kx[:, 2 * i:2 * i + 2, :]), bank(("xk", i)), slots, ("xk", i), act_copy, ("xk", i))

                keys_out(0)
                keys_out(1)
                h_highs("mix")
                keys_out(2)
                high_parts(ahead(("small", 0), 3))
                act.wait_ge(*dve_rope.at(layer, ("cos", "ik")))
                copy(small, bank(("small", 0))[:, S:S + 40].rearrange("p (c n) -> p c n", c=TILES), slots, ("small", 0), act_copy, "small")
                act.wait_ge(*act_copy.at(layer, "small"))
                nc.scalar.activation(beta, small[:, :, 12:20], ACT.Tanh, scale=0.5).then_inc(act_gdn.sem, act_gdn.mark("beta"))
                nc.scalar.activation(a_exp, param_t[:, R_ALOG:R_ALOG + 8], ACT.Exp).then_inc(act_gdn.sem, act_gdn.mark("a"))
                act.wait_ge(*dve_gate.at(layer, "abs"))
                nc.scalar.activation(ga_e, ga_abs, ACT.Exp, scale=-1.0).then_inc(act_gdn.sem, act_gdn.mark("e"))
                act.wait_ge(*dve_gate.at(layer, "w"))
                nc.scalar.activation(ga_ln, ga_w, ACT.Ln).then_inc(act_gdn.sem, act_gdn.mark("ln"))
                copy(flat(v_tok), bank(("v", 0)), slots, ("v", 0), act_copy, "v", scale=0.5)
                for c in range(TILES):
                    keys = (c + 1) * P
                    if c == 1:
                        act.wait_ge(*dve_idx.at(layer, ("score", 0)))
                    for odd in range(2):
                        what = ("logits", c, odd)
                        high_parts(ahead(what, 3))
                        act.wait_ge(*pe_idx.at(layer, what))
                        nc.scalar.activation(idx_relu[:, odd:odd + 3:2, 0:keys],
                                             bank(what)[:, 0:2 * keys].rearrange("p (h s) -> p h s", h=2), ACT.Relu)\
                            .then_inc(act_att.sem, act_att.mark(what))
                for c in range(TILES):
                    for hh in range(2):
                        what = ("decay", c, hh)
                        high_parts(ahead(what, 3))
                        act.wait_ge(*pe_gdn.at(layer, what))
                        nc.scalar.activation(flat(decay[:, 2 * c + hh, :, :]), bank(what), ACT.Exp).then_inc(act_gdn.sem, act_gdn.mark(what))
                act.wait_ge(*pe_gdn.at(layer, "g_sums"))
                nc.scalar.activation(e_last, psum[:, 7, 32:40], ACT.Exp).then_inc(act_gdn.sem, act_gdn.mark("e_last"))
                nc.scalar.activation(e_cum, psum[:, 7, 40:48], ACT.Exp).then_inc(act_gdn.sem, act_gdn.mark("e_cum"))

                def conv_last_tap(j):
                    key = CONV_SLOTS[j]
                    high_parts(ahead(key, 3))
                    act.wait_ge(*slots.at(layer, key))
                    for b in range(2):
                        nc.scalar.activation(conv[:, 2 * j + b, :], bank(key)[:, b * S:(b + 1) * S], ACT.Copy,
                                             scale=tap(3, 2 * j + b)).then_inc(act_conv.sem, act_conv.mark(("conv", j, b)))

                def conv_tanh(j):
                    act.wait_ge(*dve_conv.at(layer, ("tap", 0, j)))
                    if j >= 2:
                        act.wait_ge(*dve_conv.at(layer, ("silu", j - 2)))
                    nc.scalar.activation(th[:, j % 2, :], flat(conv[:, 2 * j:2 * j + 2, :]), ACT.Tanh, scale=0.5)\
                        .then_inc(act_conv.sem, act_conv.mark(("tanh", j)))

                def conv_square(j):
                    act.wait_ge(*dve_conv.at(layer, ("silu", j)))
                    if j >= 2:
                        act.wait_ge(*pe_gdn.at(layer, ("squares", j - 2)))
                    nc.scalar.activation(sq[:, j % 2, :], flat(conv[:, 2 * j:2 * j + 2, :]), ACT.Square)\
                        .then_inc(act_conv.sem, act_conv.mark(("sq", j)))

                def conv_step(j):
                    if j < 12:
                        conv_last_tap(j)
                    if 1 <= j <= 12:
                        conv_tanh(j - 1)
                    if 2 <= j < 10:
                        conv_square(j - 2)

                for j in range(4):
                    conv_step(j)
                for c in range(TILES):
                    keys, n_h = (c + 1) * P, 4 // (c + 1)
                    for j in range(HEADS // n_h):
                        high_parts(ahead(("scores", c, j), 3))
                        act.wait_ge(*dve_att.at(layer, ("max", c, j)))
                        for i in range(n_h):
                            hd = n_h * j + i
                            ins = nc.scalar.activation((p0, p1)[c][:, hd, :], bank(("scores", c, j))[:, i * keys:(i + 1) * keys], ACT.Exp,
                                                       bias=nmx[:, c, hd:hd + 1], scale=DH ** -0.5, accum_out=psumr[:, c, hd:hd + 1])
                        ins.then_inc(act_att.sem, act_att.mark(("scores", c, j)))
                for j in range(4, 8):
                    conv_step(j)
                for j in range(HEADS // 2):
                    copy(flat(pt0[:, 2 * j:2 * j + 2, :]), bank(("pt0", j)), pe_att, ("pt0", j), act_att, ("pt0", j))
                for j in range(HEADS // 4):
                    copy(flat(pt1[:, 4 * j:4 * j + 4, :]), bank(("pt1", j)), pe_att, ("pt1", j), act_att, ("pt1", j))
                for j in range(8, 13):
                    conv_step(j)

                def gate(part, i, block0):
                    high_parts(ahead((part, i), 3))
                    act.wait_ge(*slots.at(layer, (part, i)))
                    nc.scalar.activation(flat(gates[:, block0 + 2 * i:block0 + 2 * i + 2, :]), bank((part, i)), ACT.Tanh, scale=0.5)\
                        .then_inc(act_gate.sem, act_gate.mark((part, i)))

                for i in range(4):
                    gate("ga", i, 0)
                for i in range(4):
                    gate("gb", i, 8)
                for g in range(4):
                    copy(flat(t_low[:, g, :, :]), bank(("t_low", 1, g)), pe_gdn, ("t_low", 1, g), act_gdn, ("t_low", 1, g))
                for s in LEVELS:
                    for g in range(4):
                        copy(flat(t_up[:, g, :, :]), bank(("t_up", s, g)), pe_gdn, ("t_up", s, g), act_gdn, ("t_up", s, g))
                    if s == 8:
                        mem_highs()
                load_gain(0)
                for g in range(2):
                    copy(flat(state[:, 4 * g:4 * g + 4, :]), bank(("state", g)), pe_gdn, ("state", g), act_gdn, ("state", g))
                for g in range(4):
                    copy(flat(o_tok[:, g, :, :]), bank(("o", g)), pe_gdn, ("o", g), act_gdn, ("o", g))
                    if g >= 2:
                        act.wait_ge(*dve_gdn.at(layer, ("o", g)))
                        act.wait_ge(*dve_gdn.at(layer, ("oss", g - 2)))
                    else:
                        act.wait_ge(*act_gdn.at(layer, ("o", g)))
                        act.wait_ge(*dve_gdn.at(layer, ("rhs", 2 + g)))
                    nc.scalar.activation(th[:, g % 2, :], flat(o_tok[:, g, :, :]), ACT.Square).then_inc(act_gdn.sem, act_gdn.mark(("o_sq", g)))
                keys_out(3)
                for j in range(G_HEADS // 2):
                    act.wait_ge(*dve_gdn.at(layer, ("y", j)))
                    nc.scalar.activation(flat(y_parts[0][:, 2 * j:2 * j + 2, :]), flat(y[:, 2 * j:2 * j + 2, :]), ACT.Copy)\
                        .then_inc(act_part.sem, act_part.mark(("y", j)))
                load_pre_gain(1)
                post_and_pre_norm("mix", "out", 1, "x")
                values_out(1)
                for i in range(4):
                    copy(flat(qx[:, 2 * i:2 * i + 2, :]), bank(("xq", i)), slots, ("xq", i), act_copy, ("xq", i))
                for c in range(TILES):
                    for j in range(2):
                        high_parts(ahead(("xs", c, j), 3))
                        act.wait_ge(*dve_att.at(layer, ("xmax", c, j)))
                        for i in range(2):
                            hd = 2 * j + i
                            ins = nc.scalar.activation(px[:, c, hd, :], bank(("xs", c, j))[:, i * S:(i + 1) * S], ACT.Exp,
                                                       bias=nmx[:, c, hd:hd + 1], scale=X_DH ** -0.5, accum_out=psumr[:, c, hd:hd + 1])
                        ins.then_inc(act_att.sem, act_att.mark(("xs", c, j)))
                for j in range(2):
                    for b in range(2):
                        copy(flat(pxt[:, b, 2 * j:2 * j + 2, :]), bank(("xpt", b, j)), pe_x, ("xpt", b, j), act_att, ("xpt", b, j))
                for j in range(4):
                    copy(flat(ox[0][:, 2 * j:2 * j + 2, :]), bank(("ox", j)), pe_x, ("ox", j), act_att, ("ox", j))
                load_pre_gain(2)
                post_and_pre_norm("x", "xo", 2, "ffn")
                act.wait_ge(*dve_part.at(layer, ("h_low", "ffn", 1, 1)))
                act.dma_start(param_t[:, :], params[bass.ds(layer + 1, 1), :, :].rearrange("a p n -> p (a n)")).then_inc(param_loaded, 16)
                load_pre_gain(3)
                for i in range(FF_SLOTS):
                    high_parts(ahead(("gate", i), 3))
                    act.wait_ge(*slots.at(layer, ("gate", i)))
                    if i >= 2:
                        act.wait_ge(*dve_ff.at(layer, ("silu", i - 2)))
                    nc.scalar.activation(th[:, i % 2, :], bank(("gate", i)), ACT.Tanh, scale=0.5).then_inc(act_ff.sem, act_ff.mark(("tanh", i)))
                    high_parts(ahead(("up", i), 3))
                    if i >= 3:
                        act.wait_ge(*slots.at(layer, ("down", i - 3)))
                    act.wait_ge(*dve_ff.at(layer, ("ff", i)))
                    nc.scalar.activation(ff[0][:, i % 3, :, :].rearrange("p k t -> p (k t)"), sq[:, i % 2, :], ACT.Copy)\
                        .then_inc(act_part.sem, act_part.mark(("ff", i)))
                    if i == 3:
                        act.wait_ge(param_loaded, 16 * (layer + 2))
                        mem_highs()
                post_and_pre_norm("ffn", "down", None, None)
            act.wait_ge(param_loaded, 16 * (DEPTH + 1))
            act.wait_ge(pre_loaded, 16 * (3 * DEPTH + 1))
            act.wait_ge(gain_loaded, 16 * 3 * DEPTH)

        @block.gpsimd
        def _(pool):
            pool.wait_ge(consts_loaded, 32)
            for c in range(TILES):
                pool.wait_ge(mem_act, c + 1)
                nc.gpsimd.tensor_tensor(rs[:, c:c + 1], ss[:, c:c + 1], eps_col, ALU.add).then_inc(mem_pool, 1)
                pool.wait_ge(mem_pool, 2 * c + 1)
                nc.gpsimd.tensor_tensor(rs[:, c:c + 1], rs[:, c:c + 1], neghalf[:, 0:1], ALU.pow).then_inc(mem_pool, 1)

            lows(nc.gpsimd, 0, [0], RING, range(VECTOR_SPLITS))
            with pool.Fori(0, DEPTH) as layer:
                done = [RING]
                low_parts = lambda upto: lows(nc.gpsimd, layer, done, upto, range(VECTOR_SPLITS))

                def rsqrt(sums, r, ready, what, name, more=eps_col):
                    pool.wait_ge(*ready.at(layer, what))
                    nc.gpsimd.tensor_tensor(r, sums, more, ALU.add).then_inc(pool_norm.sem, pool_norm.mark(("mean", name)))
                    pool.wait_ge(*pool_norm.at(layer, ("mean", name)))
                    nc.gpsimd.tensor_tensor(r, r, neghalf[:, 0:1], ALU.pow).then_inc(pool_norm.sem, pool_norm.mark(name))

                def prenorm(which, more=None):
                    for c in range(TILES):
                        if more is not None:
                            low_parts(ahead(more, 3 + c))
                        rsqrt(ss[:, c:c + 1], rs[:, c:c + 1], act_norm, ("ss", which, c), ("pre", which, c))

                def postnorm(part, product):
                    if product != "down":
                        low_parts(ahead((product, 1), 2))
                        for c in range(TILES):
                            pool.wait_ge(*act_norm.at(layer, ("ss2a", part, c)))
                            nc.gpsimd.tensor_tensor(more[:, c:c + 1], ss2a[:, c:c + 1], eps_col, ALU.add)\
                                .then_inc(pool_norm.sem, pool_norm.mark(("half", part, c)))
                    for c in range(TILES):
                        low_parts(ahead(product, 1) if c == 0 else ahead((product, LAST[product]), 2))
                        if product != "down":
                            pool.wait_ge(*pool_norm.at(layer, ("half", part, c)))
                        rsqrt(ss2[:, c:c + 1], rs2[:, c:c + 1], act_norm, ("ss2", part, c), ("post", part, c),
                              eps_col if product == "down" else more[:, c:c + 1])

                prenorm("mix")
                low_parts(ahead(("kk", 0), 3))
                pool.wait_ge(*dve_gdn.at(layer, "ss"))
                nc.gpsimd.tensor_tensor(rk, ss_kq[:, :, 0:8], neghalf.rearrange("p (c h) -> p c h", c=TILES), ALU.pow)\
                    .then_inc(pool_gdn.sem, pool_gdn.mark("rk"))
                for g in range(4):
                    c, hh = g // 2, g % 2
                    o = oscale[:, c, 4 * hh:4 * hh + 4]
                    low_parts(ahead(("o", g), 2))
                    pool.wait_ge(*dve_gdn.at(layer, ("o_mean", g)))
                    nc.gpsimd.tensor_tensor(o, o, neghalf[:, 0:4], ALU.pow).then_inc(pool_gdn.sem, pool_gdn.mark(("o_scale", g)))
                low_parts(ahead(("xk", 3), 3))
                for j in range(3):
                    y_low(pool, layer, pool_part, j)
                postnorm("mix", "out")
                prenorm("x", ("out", 3))
                postnorm("x", "xo")
                prenorm("ffn")
                postnorm("ffn", "down")
                low_parts(HALVES + RING)

        @block.vector
        def _(dve):
            dve.wait_ge(consts_loaded, 32)
            for c in range(TILES):
                m = mem_block(kx_t)[:, c, :]
                dve.wait_ge(mem_pool, 2 * c + 2)
                nc.vector.tensor_scalar(m, m, rs[:, c:c + 1], None, ALU.mult).then_inc(mem_dve, 1)
            dve.wait_ge(pos_loaded, 16)
            pos = y_t[:, S:2 * S]
            nc.vector.tensor_copy(pos, y_t[:, 0:S].bitcast(I32)).then_inc(table.sem, table.mark("pos"))
            dve.wait_ge(*table.at(0, "pos"))
            ang, turns = rb_t[:, 0:S], rb_t[:, S:2 * S]
            for w, inv, sgn in ((0, C_INV_A, C_SGN_A), (2, C_INV_I, C_SGN_I)):
                r = angle(w + 1)

                def then(ins, name):
                    ins.then_inc(table.sem, table.mark((name, w)))
                    dve.wait_ge(*table.at(0, (name, w)))

                then(nc.vector.tensor_scalar(ang, pos, const_t[:, inv:inv + 1], None, ALU.mult), "ang")
                then(nc.vector.tensor_scalar(turns, ang, 1 / (2 * PI), ROUND, ALU.mult, ALU.add), "round")
                then(nc.vector.tensor_scalar(turns, turns, ROUND, None, ALU.subtract), "turns")
                for n, part in enumerate((TWO_PI_1, TWO_PI_2, TWO_PI_3)):
                    then(nc.vector.scalar_tensor_tensor(out=ang, in0=turns, scalar=-part, in1=ang, op0=ALU.mult, op1=ALU.add), f"less{n}")
                then(nc.vector.tensor_scalar(ang, ang, PI_BELOW, -PI_BELOW, ALU.min, ALU.max), "clamp")
                nc.vector.tensor_scalar(r, ang, const_t[:, sgn:sgn + 1], None, ALU.mult).then_inc(table.sem, table.mark(("angle", w + 1)))
                then(nc.vector.scalar_tensor_tensor(out=turns, in0=ang, scalar=-1.0, in1=ang, op0=ALU.mult, op1=ALU.max), "abs")
                nc.vector.tensor_scalar(angle(w), turns, -1.0, PI / 2, ALU.mult, ALU.add).then_inc(table.sem, table.mark(("angle", w)))
                dve.wait_ge(*table.at(0, ("angle", w)))
            dve.wait_ge(x_loaded, 16)
            for c in range(TILES):
                nc.vector.memset(top8[:, c:c + 1], 0.0).then_inc(x_ready, 1)
            dve.wait_ge(x_ready, TILES)

            V = nc.vector

            def mem_lows():
                for k in range(KT):
                    ins = V.scalar_tensor_tensor(out=mem_gain[1][:, k, :], in0=mem_feat[:, k, :], scalar=param_t[:, R_MEM + k:R_MEM + k + 1],
                                                 in1=mem_gain[0][:, k, :].bitcast(F32), op0=ALU.mult, op1=ALU.subtract)
                ins.then_inc(mem_low_ready, 1)

            lows(V, 0, [0], RING, range(VECTOR_SPLITS, RING))
            dve.wait_ge(mem_high_ready, 1)
            mem_lows()
            with dve.Fori(0, DEPTH) as layer:
                done = [RING]
                low_parts = lambda upto: lows(V, layer, done, upto, range(VECTOR_SPLITS, RING))

                def link(ins, done, name):
                    ins.then_inc(done.sem, done.mark(name))
                    dve.wait_ge(*done.at(layer, name))

                def prenorm(which, row):
                    dve.wait_ge(pre_loaded, 16 * (3 * layer + row + 1))
                    for c in range(TILES):
                        dve.wait_ge(*pool_norm.at(layer, ("pre", which, c)))
                        V.scalar_tensor_tensor(out=xn[:, c, :], in0=x[:, c, :], scalar=rs[:, c:c + 1], in1=pre_gain_t[:, :], op0=ALU.mult, op1=ALU.mult)\
                            .then_inc(dve_norm.sem, dve_norm.mark(("xn", which, c)))
                    for c in range(TILES):
                        for half in range(2):
                            what = ("h", which, c, half)
                            low_parts(ahead(what, 2))
                            dve.wait_ge(*act_part.at(layer, what))
                            to = slice(4 * half, 4 * half + 4), slice(c * P, (c + 1) * P)
                            V.tensor_tensor(h[1][:, to[0], to[1]], bank(what).rearrange("p (k t) -> p k t", k=4),
                                            h[0][:, to[0], to[1]].bitcast(F32), ALU.subtract).then_inc(dve_part.sem, dve_part.mark(("h_low", which, c, half)))

                def postnorm(part, product, row, final=False):
                    start = 0 if product == "down" else 512
                    if start:
                        low_parts(ahead((product, 1), 2))
                        dve.wait_ge(gain_loaded, 16 * (3 * layer + row + 1))
                        for c in range(TILES):
                            dve.wait_ge(*act_norm.at(layer, ("ss2a", part, c)))
                            V.tensor_tensor(xn[:, c, 0:start], y_tile(c)[:, 0:start], gain_t[:, 0:start], ALU.mult)\
                                .then_inc(dve_norm.sem, dve_norm.mark(("scaled_a", part, c)))
                    for c in range(TILES):
                        low_parts(ahead(product, 1) if c == 0 else ahead((product, LAST[product]), 2))
                        if c == 0:
                            dve.wait_ge(gain_loaded, 16 * (3 * layer + row + 1))
                        dve.wait_ge(*act_norm.at(layer, ("ss2", part, c)))
                        V.tensor_tensor(xn[:, c, start:D], y_tile(c)[:, start:D], gain_t[:, start:D], ALU.mult)\
                            .then_inc(dve_norm.sem, dve_norm.mark(("scaled", part, c)))
                    for c in range(TILES):
                        dve.wait_ge(*dve_norm.at(layer, ("scaled", part, 1)))
                        dve.wait_ge(*pool_norm.at(layer, ("post", part, c)))
                        ins = V.scalar_tensor_tensor(out=x[:, c, :], in0=xn[:, c, :], scalar=rs2[:, c:c + 1], in1=x[:, c, :],
                                                     op0=ALU.mult, op1=ALU.add)
                        if final:
                            ins.then_inc(x_ready, 1)
                        else:
                            ins.then_inc(dve_norm.sem, dve_norm.mark(("x", part, c)))
                            if part == "mix":
                                low_parts(ahead((product, LAST[product]), 3 + c))

                def rotate(what, key, out, blocks, cos, half, name, buf):
                    src = bank(key)[:, 0:blocks * S].rearrange("p (b t) -> p b t", b=blocks)
                    tmp = rope_tmp[:, buf, 0:blocks * S].rearrange("p (b t) -> p b t", b=blocks)
                    low_parts(ahead(key, 2))
                    dve.wait_ge(*slots.at(layer, key))
                    for lo in range(0, P, half):
                        o = lo ^ half
                        V.tensor_tensor(tmp[lo:lo + half], src[o:o + half],
                                        rope[o:o + half, cos + 1, :].unsqueeze(1).broadcast_to([half, blocks, S]), ALU.mult)\
                            .then_inc(dve_rope.sem, dve_rope.mark(("partner", name, lo)))
                    link(V.tensor_tensor(out, src, heads(rope[:, cos, :], blocks), ALU.mult), dve_rope, ("cos", name))
                    link(V.tensor_tensor(out, out, tmp, ALU.add), dve_rope, name)

                prenorm("mix", 0)
                dve.wait_ge(tables_act, 4)
                rotate("iq", ("iq", 0), iq, 2, 2, 32, "iq", 0)
                rotate("ik", ("small", 0), ik.unsqueeze(1), 1, 2, 32, "ik", 1)
                dve.wait_ge(*act_copy.at(layer, "small"))
                link(V.tensor_tensor(ga_x, small[:, :, 4:12], heads(param_t[:, R_DT:R_DT + 8], TILES), ALU.add), dve_gate, "x")
                link(V.scalar_tensor_tensor(out=ga_abs, in0=ga_x, scalar=-1.0, in1=ga_x, op0=ALU.mult, op1=ALU.max), dve_gate, "abs")
                dve.wait_ge(*act_gdn.at(layer, "e"))
                link(V.tensor_scalar(ga_w, ga_e, 1.0, None, ALU.add), dve_gate, "w")
                link(V.scalar_tensor_tensor(out=ga_t, in0=ga_w, scalar=-1.0, in1=ga_e, op0=ALU.add, op1=ALU.subtract), dve_gate, "t")
                link(V.reciprocal(ga_r, ga_w), dve_gate, "r")
                link(V.tensor_tensor(ga_t, ga_t, ga_r, ALU.mult), dve_gate, "t2")
                dve.wait_ge(*act_gdn.at(layer, "ln"))
                link(V.tensor_tensor(ga_t, ga_ln, ga_t, ALU.subtract), dve_gate, "log1p")
                link(V.scalar_tensor_tensor(out=ga_t, in0=ga_x, scalar=0.0, in1=ga_t, op0=ALU.max, op1=ALU.add), dve_gate, "softplus")
                link(V.scalar_tensor_tensor(out=g_tok, in0=ga_t, scalar=-1.0, in1=heads(a_exp, TILES), op0=ALU.mult, op1=ALU.mult), dve_gate, "g")
                link(V.tensor_scalar(beta, beta, 0.5, 0.5, ALU.mult, ALU.add), dve_gate, "beta")
                V.tensor_scalar(half_gdn, param_t[:, R_GDN:R_GDN + 1], 0.5, None, ALU.mult).then_inc(dve_gate.sem, dve_gate.mark("half_gdn"))
                for c in range(TILES):
                    V.tensor_tensor(g_after[:, c, :, :], heads(after, G_HEADS), cols(g_tok[:, c, :], P), ALU.mult)\
                        .then_inc(dve_gate.sem, dve_gate.mark(("g_after", c)))
                rotate("k", ("k", 0), kT, 2, 0, 64, "k", 0)
                rotate("q0", ("q", 0), q[:, 0:2, :], 2, 0, 64, ("q", 0), 1)
                for c in range(TILES):
                    keys = (c + 1) * P
                    val = idx_val[:, c, 0:keys]
                    diag = idx_val[:, c, c * P:(c + 1) * P]
                    low_parts(ahead(("logits", c, 1), 2))
                    dve.wait_ge(*act_att.at(layer, ("logits", c, 0)))
                    dve.wait_ge(*act_att.at(layer, ("logits", c, 1)))
                    link(V.tensor_scalar(val, idx_relu[:, 0, 0:keys], small[:, c, 0:1], None, ALU.mult), dve_idx, ("w0", c))
                    for hd in range(1, IDX_HEADS):
                        link(V.scalar_tensor_tensor(out=val, in0=idx_relu[:, hd, 0:keys], scalar=small[:, c, hd:hd + 1], in1=val,
                                                    op0=ALU.mult, op1=ALU.add), dve_idx, ("score", c) if hd == 3 else ("w", c, hd))
                    V.tensor_tensor(diag, diag, idx_bias, ALU.add)
                    for n in range(TOPK // 8):
                        low_parts(min(ahead(("logits", 0, 1), 2 + (8 * c + n) // 3), ahead(("bk", 1), 3)))
                        dve.drain()
                        V.max(top8, val)
                        dve.drain()
                        V.match_replace(val, top8, val, TAKEN)
                    dve.drain()
                    link(V.tensor_scalar(sel_bias[:, c, 0:keys], val, TAKEN / 2, NEG, ALU.is_gt, ALU.mult), dve_idx, ("sel", c))
                    sel_diag = sel_bias[:, c, c * P:(c + 1) * P]
                    link(V.tensor_tensor(sel_diag, sel_diag, idx_bias, ALU.min), dve_idx, ("bias", c))
                for i in range(1, 4):
                    rotate("q", ("q", i), q[:, 2 * i:2 * i + 2, :], 2, 0, 64, ("q", i), (i + 1) % 2)

                def conv_taps(j):
                    low_parts(ahead(CONV_SLOTS[j], 2))
                    for d in range(1, CONV_K):
                        for b in range(2):
                            blk = 2 * j + b
                            if d == 1:
                                dve.wait_ge(*act_conv.at(layer, ("conv", j, 1)))
                            else:
                                dve.wait_ge(*dve_conv.at(layer, ("tap" if b else "tap_a", 4 - d, j)))
                            V.scalar_tensor_tensor(out=conv[:, blk, d:S], in0=bank(CONV_SLOTS[j])[:, b * S:(b + 1) * S - d],
                                                   scalar=tap(3 - d, blk), in1=conv[:, blk, d:S], op0=ALU.mult, op1=ALU.add)\
                                .then_inc(dve_conv.sem, dve_conv.mark(("tap" if b else "tap_a", 3 - d, j)))

                def conv_silu(j):
                    c2 = flat(conv[:, 2 * j:2 * j + 2, :])
                    dve.wait_ge(*act_conv.at(layer, ("tanh", j)))
                    V.scalar_tensor_tensor(out=c2, in0=th[:, j % 2, :], scalar=1.0, in1=c2, op0=ALU.add, op1=ALU.mult)\
                        .then_inc(dve_conv.sem, dve_conv.mark(("silu", j)))

                def conv_step(j):
                    if j < 12:
                        conv_taps(j)
                    if j >= 1:
                        conv_silu(j - 1)

                def row_max(scores, c, h0, n_h, scale, name):
                    link(V.tensor_reduce(mx[:, c, h0:h0 + n_h], scores, AX_X, ALU.max), dve_att, ("mx", name))
                    V.tensor_scalar(nmx[:, c, h0:h0 + n_h], mx[:, c, h0:h0 + n_h], -scale, None, ALU.mult)\
                        .then_inc(dve_att.sem, dve_att.mark(name))

                def normalise(pr, c, h0, n_h, name):
                    link(V.reciprocal(pinv[:, c, h0:h0 + n_h], psumr[:, c, h0:h0 + n_h]), dve_att, ("inv", name))
                    V.tensor_tensor(pr, pr, cols(pinv[:, c, h0:h0 + n_h], pr.shape[-1]), ALU.mult)\
                        .then_inc(dve_att.sem, dve_att.mark(name))

                for j in range(4):
                    conv_step(j)
                for c in range(TILES):
                    keys, n_h = (c + 1) * P, 4 // (c + 1)
                    for j in range(HEADS // n_h):
                        low_parts(ahead(("scores", c, j), 2))
                        dve.wait_ge(*pe_att.at(layer, ("scores", c, j)))
                        row_max(bank(("scores", c, j)).rearrange("p (h s) -> p h s", h=n_h), c, n_h * j, n_h, DH ** -0.5, ("max", c, j))
                for j in range(4, 6):
                    conv_step(j)
                for c in range(TILES):
                    n_h = 4 // (c + 1)
                    for j in range(HEADS // n_h):
                        dve.wait_ge(*act_att.at(layer, ("scores", c, j)))
                        normalise((p0, p1)[c][:, n_h * j:n_h * (j + 1), :], c, n_h * j, n_h, ("p", c, j))
                for j in range(6, 11):
                    conv_step(j)
                low_parts(ahead(("squares", 7), 2))
                dve.wait_ge(*pe_gdn.at(layer, ("squares", 7)))
                link(V.tensor_scalar(ss_kq, psum[:, 7, 0:32].rearrange("p (c b) -> p c b", c=TILES), 4 * EPS, None, ALU.add), dve_gdn, "ss")
                for j in range(11, 13):
                    conv_step(j)
                V.tensor_scalar(o_eps, ss_kq[:, :, 8:16], DH * EPS, None, ALU.mult).then_inc(dve_gdn.sem, dve_gdn.mark("o_eps"))
                dve.wait_ge(*pool_gdn.at(layer, "rk"))
                dve.wait_ge(*act_gdn.at(layer, "e_last"))
                V.scalar_tensor_tensor(out=v_scale, in0=ss_kq[:, :, 0:8], scalar=0.5, in1=rk, op0=ALU.mult, op1=ALU.mult)\
                    .then_inc(dve_gdn.sem, dve_gdn.mark("v_scale"))
                V.tensor_tensor(k_scale0, rk[:, 0, :], e_last, ALU.mult).then_inc(dve_gdn.sem, dve_gdn.mark("k_scale0"))
                link(V.tensor_tensor(d_k, beta, rk, ALU.mult), dve_gdn, "d_k")
                link(V.tensor_tensor(m_scale, d_k, rk, ALU.mult), dve_gdn, "m_scale")
                for g in range(4):
                    c, hh = g // 2, g % 2
                    low_parts(ahead(("kk", g), 2))
                    dve.wait_ge(*act_gdn.at(layer, ("decay", c, hh)))
                    for kind, dst, scale in (("kk", m_up, m_scale), ("kq", attn, rk)):
                        low_parts(ahead((kind, g), 2))
                        dve.wait_ge(*pe_gdn.at(layer, (kind, g)))
                        for i in range(4):
                            ins = V.scalar_tensor_tensor(out=dst[:, g, i, :], in0=bank((kind, g))[:, i * P:(i + 1) * P],
                                                         scalar=scale[:, c, 4 * hh + i:4 * hh + i + 1], in1=decay[:, g, i, :],
                                                         op0=ALU.mult, op1=ALU.mult)
                        ins.then_inc(dve_gdn.sem, dve_gdn.mark((kind, g)))
                    dve.wait_ge(*dve_gdn.at(layer, ("kk", g)))
                    link(V.tensor_tensor(t_up[:, g, :, :], m_up[:, g, :, :], heads(mask1, 4), ALU.mult), dve_gdn, ("m1", g))
                    V.scalar_tensor_tensor(out=t_up[:, g, :, :], in0=t_up[:, g, :, :], scalar=-1.0, in1=heads(ident, 4),
                                           op0=ALU.mult, op1=ALU.add).then_inc(dve_gdn.sem, dve_gdn.mark(("t_up", g)))
                for j in range(HEADS // 2):
                    low_parts(ahead(("ga", j), 2))
                    dve.wait_ge(*act_gate.at(layer, ("ga", j)))
                    low_parts(ahead(("att", j), 2))
                    dve.wait_ge(*pe_att.at(layer, ("att", j)))
                    V.scalar_tensor_tensor(out=flat(y[:, 2 * j:2 * j + 2, :]), in0=flat(gates[:, 2 * j:2 * j + 2, :]), scalar=1.0,
                                           in1=bank(("att", j)), op0=ALU.add, op1=ALU.mult).then_inc(dve_att.sem, dve_att.mark(("att", j)))

                def by_head(out, what, scale, name):
                    low_parts(ahead(what, 2))
                    dve.wait_ge(*pe_gdn.at(layer, what))
                    V.tensor_tensor(out, bank(what).rearrange("p (h n) -> p h n", h=4), cols(scale, P), ALU.mult)\
                        .then_inc(dve_gdn.sem, dve_gdn.mark(name))

                for g in range(4):
                    by_head(rhs[:, g, :, :], ("v_tok", g), v_scale[:, g // 2, 4 * (g % 2):4 * (g % 2) + 4], ("v_tok", g))
                for g in range(2):
                    by_head(k_dec[:, 4 * g:4 * g + 4, :], ("k_tok", g), k_scale0[:, 4 * g:4 * g + 4], ("k_tok", g))
                for n, s in enumerate(LEVELS):
                    level_mask = const_t[:, C_LEVEL + 64 * n:C_LEVEL + 64 * (n + 1)]
                    for g in range(4):
                        low_parts(ahead(("mt", s, g), 2))
                        dve.wait_ge(*pe_gdn.at(layer, ("mt", s, g)))
                        V.tensor_tensor(prod[:, g, :, :], bank(("mt", s, g))[:, 0:256].rearrange("p (h n) -> p h n", h=4),
                                        heads(level_mask, 4), ALU.mult).then_inc(dve_gdn.sem, dve_gdn.mark(("mt", s, g)))
                    for g in range(4):
                        low_parts(ahead(("tmt", s, g), 2))
                        dve.wait_ge(*pe_gdn.at(layer, ("tmt", s, g)))
                        t = even(t_low[:, g, :, :], s)
                        V.tensor_tensor(t, t, bank(("tmt", s, g))[:, 0:256].rearrange("p (b c) -> p b c", c=s), ALU.subtract)\
                            .then_inc(dve_gdn.sem, dve_gdn.mark(("t_low", s, g)))
                for g in range(2):
                    by_head(v_new[:, g, :, :], ("solved", g), d_k[:, 0, 4 * g:4 * g + 4], ("v_new", g))
                for g in range(2):
                    pred = th[:, g, :].rearrange("p (h n) -> p h n", h=4)
                    by_head(pred, ("ks", g), e_cum[:, 4 * g:4 * g + 4], ("ks", g))
                    dve.wait_ge(*dve_gdn.at(layer, ("ks", g)))
                    V.tensor_tensor(rhs[:, 2 + g, :, :], rhs[:, 2 + g, :, :], pred, ALU.subtract).then_inc(dve_gdn.sem, dve_gdn.mark(("rhs", 2 + g)))
                for g in range(2):
                    by_head(sq[:, g, :].rearrange("p (h n) -> p h n", h=4), ("qs", g), e_cum[:, 4 * g:4 * g + 4], ("qs", g))
                for g in range(2):
                    by_head(v_new[:, 2 + g, :, :], ("solved", 2 + g), d_k[:, 1, 4 * g:4 * g + 4], ("v_new", 2 + g))
                for g in range(4):
                    c, hh = g // 2, g % 2
                    s4 = slice(4 * hh, 4 * hh + 4)
                    if g >= 2:
                        dve.wait_ge(*act_gdn.at(layer, ("o", g)))
                        V.tensor_tensor(flat(o_tok[:, g, :, :]), flat(o_tok[:, g, :, :]), sq[:, g % 2, :], ALU.add)\
                            .then_inc(dve_gdn.sem, dve_gdn.mark(("o", g)))
                    dve.wait_ge(*act_gdn.at(layer, ("o_sq", g)))
                    link(V.tensor_reduce(oss[:, c, s4], th[:, g % 2, :].rearrange("p (h n) -> p h n", h=4), AX_X, ALU.add), dve_gdn, ("oss", g))
                    V.scalar_tensor_tensor(out=oscale[:, c, s4], in0=oss[:, c, s4], scalar=1.0 / DH, in1=o_eps[:, c, s4],
                                           op0=ALU.mult, op1=ALU.add).then_inc(dve_gdn.sem, dve_gdn.mark(("o_mean", g)))
                for g in range(4):
                    c, hh = g // 2, g % 2
                    dve.wait_ge(*pool_gdn.at(layer, ("o_scale", g)))
                    V.tensor_tensor(o_tok[:, g, :, :], o_tok[:, g, :, :], cols(oscale[:, c, 4 * hh:4 * hh + 4], P), ALU.mult)\
                        .then_inc(dve_gdn.sem, dve_gdn.mark(("o_norm", g)))
                for j in range(G_HEADS // 2):
                    low_parts(ahead(("yb", j), 2))
                    dve.wait_ge(*pe_gdn.at(layer, ("yb", j)))
                    dve.wait_ge(*act_gate.at(layer, ("gb", j)))
                    link(V.scalar_tensor_tensor(out=th[:, j % 2, :], in0=flat(gates[:, 8 + 2 * j:10 + 2 * j, :]), scalar=1.0,
                                                in1=bank(("yb", j)), op0=ALU.add, op1=ALU.mult), dve_gdn, ("yb", j))
                    y2 = flat(y[:, 2 * j:2 * j + 2, :])
                    V.scalar_tensor_tensor(out=y2, in0=th[:, j % 2, :], scalar=half_gdn, in1=y2, op0=ALU.mult, op1=ALU.add)\
                        .then_inc(dve_gdn.sem, dve_gdn.mark(("y", j)))
                y_low(dve, layer, dve_part, 3)
                postnorm("mix", "out", 0)
                prenorm("x", 1)
                for c in range(TILES):
                    for j in range(2):
                        low_parts(ahead(("xs", c, j), 2))
                        dve.wait_ge(*pe_x.at(layer, ("xs", c, j)))
                        row_max(bank(("xs", c, j)).rearrange("p (h s) -> p h s", h=2), c, 2 * j, 2, X_DH ** -0.5, ("xmax", c, j))
                for c in range(TILES):
                    for j in range(2):
                        dve.wait_ge(*act_att.at(layer, ("xs", c, j)))
                        normalise(px[:, c, 2 * j:2 * j + 2, :], c, 2 * j, 2, ("px", c, j))
                for j in range(4):
                    low_parts(ahead(("ox", j), 2))
                    dve.wait_ge(*act_att.at(layer, ("ox", j)))
                    V.tensor_tensor(flat(ox[1][:, 2 * j:2 * j + 2, :]), bank(("ox", j)), flat(ox[0][:, 2 * j:2 * j + 2, :]).bitcast(F32), ALU.subtract)\
                        .then_inc(dve_part.sem, dve_part.mark(("ox_low", j)))
                postnorm("x", "xo", 1)
                prenorm("ffn", 2)
                for i in range(FF_SLOTS):
                    low_parts(ahead(("gate", i), 2))
                    dve.wait_ge(*act_ff.at(layer, ("tanh", i)))
                    link(V.scalar_tensor_tensor(out=sq[:, i % 2, :], in0=th[:, i % 2, :], scalar=1.0, in1=bank(("gate", i)),
                                                op0=ALU.add, op1=ALU.mult), dve_ff, ("silu", i))
                    low_parts(ahead(("up", i), 2))
                    dve.wait_ge(*slots.at(layer, ("up", i)))
                    V.scalar_tensor_tensor(out=sq[:, i % 2, :], in0=sq[:, i % 2, :], scalar=0.5, in1=bank(("up", i)),
                                           op0=ALU.mult, op1=ALU.mult).then_inc(dve_ff.sem, dve_ff.mark(("ff", i)))
                    dve.wait_ge(*act_part.at(layer, ("ff", i)))
                    V.tensor_tensor(ff[1][:, i % 3, :, :].rearrange("p k t -> p (k t)"), sq[:, i % 2, :],
                                    ff[0][:, i % 3, :, :].rearrange("p k t -> p (k t)").bitcast(F32), ALU.subtract)\
                        .then_inc(dve_part.sem, dve_part.mark(("ff_low", i)))
                    if i == 3:
                        dve.wait_ge(mem_high_ready, 2 * layer + 3)
                        mem_lows()
                postnorm("ffn", "down", 2, final=True)
                low_parts(HALVES + RING)


CONV_SLOTS = [(part, i) for part in ("bk", "bq", "bv") for i in range(4)]
LAST = {"out": 3, "xo": 3, "down": FF_SLOTS - 1}


def mem_block(t):
    return t[:, :].rearrange("p (c d) -> p c d", c=TILES)


def flat(ap):
    return ap.rearrange("p a b -> p (a b)")


def constants():
    i = np.arange(P)
    c = np.zeros((P, N_CONST), np.float32)
    c[:, C_IDENT:C_IDENT + P] = np.eye(P)
    c[:, C_AFTER:C_AFTER + P] = i[:, None] > i[None, :]
    c[:, C_UPTO:C_UPTO + P] = i[:, None] <= i[None, :]
    c[:, C_MASK1:C_MASK1 + P] = (i[None, :] == i[:, None] + 1) & (i[:, None] % 2 == 0)
    c[:, C_IDXBIAS:C_IDXBIAS + P] = np.where(i[None, :] > i[:, None], NEG, 0.0)
    for n, s in enumerate(LEVELS):
        k = np.concatenate([np.arange(2 * s * b, 2 * s * b + s) for b in range(P // (2 * s))])
        c[:, C_LEVEL + 64 * n:C_LEVEL + 64 * (n + 1)] = i[:, None] // s == k[None, :] // s + 1
    for col, sgn, d in ((C_INV_A, C_SGN_A, DH), (C_INV_I, C_SGN_I, IDX_DIM)):
        inv = np.float32(THETA) ** (-np.arange(d // 2, dtype=np.float32) * np.float32(2) / np.float32(d))
        c[:, col] = inv[i % (d // 2)]
        c[:, sgn] = np.where(i % d < d // 2, 1.0, -1.0)
    c[:, C_ONE] = 1.0
    c[:, C_EPS] = EPS
    c[:, C_NEGHALF:] = -0.5
    b = np.zeros((P, 5 * P), np.float32)
    b[:, 0:P] = np.eye(P)
    b[:, P:] = np.tile(np.where(i[None, :] < i[:, None], NEG, 0.0), (1, 4))
    return c, b.astype(mybir.dt.np(BF16))


def lay_out(inputs):
    w = {k: np.asarray(v) for k, v in inputs.items()}
    stream = np.zeros((DEPTH, HALVES, P, HALF), np.float32)

    def blocks(m):
        return m.reshape(-1, P, m.shape[1]).transpose(1, 0, 2)

    for layer in range(DEPTH):
        w_in = w["w_in"][layer]
        part = lambda name: w_in[:, COL[name]:COL[name] + SIZES[name]]
        tokenwise = np.concatenate([part("iw"), part("ba"), part("bb")], 1)
        mats = {**{k: part(k) for k in ("iq", "k", "q", "bq", "bk", "bv", "ga", "gb")},
                "xk": w["w_xkv"][layer][:, 0:D], "xq": w["w_xq"][layer],
                "gate": w["w_gu"][layer][:, 0:FF], "up": w["w_gu"][layer][:, FF:]}
        tall = {"out": w["w_out"][layer], "xo": w["w_xo"][layer], "xv": w["w_xkv"][layer][:, D:]}
        for (name, i), n in HALF_AT.items():
            for b in range(2):
                to = stream[layer, n + b]
                if name == "small":
                    piece = blocks(np.concatenate([part("ik"), part("ik")], 1) if b == 0 else tokenwise)
                    to.reshape(P, KT, P)[:, :, 0:piece.shape[2]] = piece
                elif name == "v":
                    to[:] = blocks(part("v")[512 * b:512 * (b + 1)]).reshape(P, HALF)
                elif name == "down":
                    to[:] = w["w_down"][layer][256 * i + P * b:256 * i + P * (b + 1)]
                elif name in tall:
                    row = 512 * (i % 2) + 256 * b
                    to[:] = blocks(tall[name][row:row + 256, 512 * (i // 2):512 * (i // 2 + 1)]).reshape(P, HALF)
                else:
                    col = 256 * i + P * b
                    to[:] = blocks(mats[name][:, col:col + P]).reshape(P, HALF)
    params = np.zeros((DEPTH + 1, P, N_PARAM), np.float32)
    for layer in range(DEPTH):
        p = params[layer]
        taps = w["conv_w"][layer].reshape(CONV_K, 3, D)[:, [1, 0, 2]]
        p[:, R_CONV:R_CONV + 96] = taps.reshape(CONV_K * 24, P).T
        p[:, R_MEM:R_MEM + KT] = w["norm_mem"][layer].reshape(KT, P).T
        p[:, R_GDN] = w["gdn_norm"][layer]
        p[:, R_DT:R_DT + 8] = w["dt_bias"][layer][None, :]
        p[:, R_ALOG:R_ALOG + 8] = w["a_log"][layer][None, :]
    post = np.zeros((3 * DEPTH, D), np.float32)
    pre = np.zeros((3 * DEPTH + 1, D), np.float32)
    for layer in range(DEPTH):
        for row, name in enumerate(("norm_mix_pre", "norm_x_pre", "norm_ffn_pre")):
            pre[3 * layer + row] = w[name][layer]
        for row, name in enumerate(("norm_mix_post", "norm_x_post", "norm_ffn_post")):
            post[3 * layer + row] = w[name][layer]
    return np.concatenate([stream.reshape(DEPTH * HALVES, P, HALF), np.zeros((RING, P, HALF), np.float32)]), params, pre, post


def kernel(**inputs):
    import concourse.bacc as bacc
    from concourse.bass_utils import run_bass_kernel_spmd

    weights, params, pre, post = lay_out(inputs)
    consts, consts_b = constants()
    arrays = {"x": np.asarray(inputs["x"])[0], "mem": np.asarray(inputs["mem"])[0], "positions": np.asarray(inputs["positions"]),
              "weights": weights, "params": params, "pre_gains": pre, "post_gains": post, "consts": consts, "consts_b": consts_b}
    plan = Plan()
    for _ in range(2):
        nc = bacc.Bacc("TRN2", target_bir_lowering=False, num_devices=1)
        args = [nc.dram_tensor(n, a.shape, mybir.dt.from_np(a.dtype), kind="ExternalInput").ap() for n, a in arrays.items()]
        out = nc.dram_tensor("out", (S, D), F32, kind="ExternalOutput").ap()
        nc.disable_value_cache = True
        program(nc, plan, *args, out)
    r = run_bass_kernel_spmd(nc, [arrays], core_ids=[0])
    return r.results[0]["out"][None]
```
